# Optimizing a Trainium2 kernel written in Bass

```python
import jax
import jax.numpy as jnp
from jax import lax
import numpy as np

D_MODEL = 1024
BATCH = 1
SEQ = 1024
DEPTH = 1
DEC_BATCH = 1
DEC_SEQ = 64
PAST_LEN = 512

CHUNK = 64
WINDOW = 128
WINDOW_CHUNKS = WINDOW // CHUNK
D_MIX = D_MODEL
ATT_WIDTH = D_MIX // 2
N_ATT_HEADS = 8
HEAD_DIM = ATT_WIDTH // N_ATT_HEADS
N_KV_HEADS = 2
GQA_GROUP = N_ATT_HEADS // N_KV_HEADS
LSTM_WIDTH = D_MIX - ATT_WIDTH
N_LSTM_HEADS = 4
LSTM_HEAD_DIM = LSTM_WIDTH // N_LSTM_HEADS
PROJ_WIDTHS = (ATT_WIDTH, N_KV_HEADS * HEAD_DIM, N_KV_HEADS * HEAD_DIM,
               LSTM_WIDTH, LSTM_WIDTH, LSTM_WIDTH, LSTM_WIDTH, N_LSTM_HEADS, N_LSTM_HEADS)
D_IN_PROJ = sum(PROJ_WIDTHS)
D_FF = 2816
EPS = 1e-6

kernel_name = "hymba_swa_sink_mlstm_macaron_step"

def _rmsnorm(x, g):
    xf = x.astype(jnp.float32)
    y = xf * lax.rsqrt(jnp.mean(xf * xf, axis=-1, keepdims=True) + EPS)
    return (y * g.astype(jnp.float32)).astype(x.dtype)

def _swiglu_half(x, g, w_gate, w_up, w_down):
    h = _rmsnorm(x, g)
    return 0.5 * ((jax.nn.silu(h @ w_gate) * (h @ w_up)) @ w_down)

def _alibi_slopes():
    h = jnp.arange(1, N_ATT_HEADS + 1, dtype=jnp.float32)
    return jnp.exp2(-8.0 * h / N_ATT_HEADS).reshape(N_KV_HEADS, GQA_GROUP)

def _in_proj(x, g_mix, w_in, b_i, b_f):
    h = _rmsnorm(x, g_mix)
    z = h @ w_in
    q, k, v, mq, mk, mv, mo, ig, fg = jnp.split(z, np.cumsum(PROJ_WIDTHS)[:-1].tolist(), axis=-1)
    lead = x.shape[:-1]
    return (q.reshape(lead + (N_ATT_HEADS, HEAD_DIM)),
            k.reshape(lead + (N_KV_HEADS, HEAD_DIM)),
            v.reshape(lead + (N_KV_HEADS, HEAD_DIM)),
            mq.reshape(lead + (N_LSTM_HEADS, LSTM_HEAD_DIM)),
            mk.reshape(lead + (N_LSTM_HEADS, LSTM_HEAD_DIM)),
            mv.reshape(lead + (N_LSTM_HEADS, LSTM_HEAD_DIM)),
            mo.reshape(lead + (N_LSTM_HEADS, LSTM_HEAD_DIM)),
            (ig + b_i).astype(jnp.float32),
            jax.nn.log_sigmoid((fg + b_f).astype(jnp.float32)))

def _sink_attention(q, k, v, dist, valid, sinks):
    s = jnp.einsum("bcqkgd,bcskd->bckgqs", q, k).astype(jnp.float32) * (HEAD_DIM ** -0.5)
    s = s - _alibi_slopes()[:, :, None, None] * dist.astype(jnp.float32)
    s = jnp.where(valid[None, :, None, None, None, :], s, -jnp.inf)
    sink = sinks.astype(jnp.float32).reshape(N_KV_HEADS, GQA_GROUP, 1)
    mx = jnp.maximum(jnp.max(s, axis=-1), sink)
    p = jnp.exp(s - mx[..., None])
    den = jnp.sum(p, axis=-1) + jnp.exp(sink - mx)
    w = (p / den[..., None]).astype(v.dtype)
    return jnp.einsum("bckgqs,bcskd->bcqkgd", w, v)

def _mlstm_scan(q, k, v, log_i, log_f, C0, n0, m0, block):
    bsz, seq = q.shape[:2]
    nb = seq // block

    def blocks(t):
        t = t.astype(jnp.float32).reshape((bsz, nb, block) + t.shape[2:])
        return jnp.moveaxis(t, 1, 0)

    xs = (blocks(q), blocks(k * (LSTM_HEAD_DIM ** -0.5)), blocks(v), blocks(log_i), blocks(log_f))
    causal = jnp.tril(jnp.ones((block, block), dtype=bool))

    def step(carry, inp):
        C, n, m = carry
        qc, kc, vc, ic, fc = inp
        b = jnp.cumsum(fc, axis=1)
        d = b[:, :, None, :] - b[:, None, :, :] + ic[:, None, :, :]
        d = jnp.where(causal[None, :, :, None], d, -jnp.inf)
        inter = b + m[:, None, :]
        mt = jnp.maximum(inter, jnp.max(d, axis=2))
        a = jnp.exp(d - mt[:, :, None, :]) * jnp.einsum("bthd,bshd->btsh", qc, kc)
        w_inter = jnp.exp(inter - mt)
        num = (jnp.einsum("btsh,bshd->bthd", a, vc)
               + w_inter[..., None] * jnp.einsum("bthd,bhde->bthe", qc, C))
        den = jnp.sum(a, axis=2) + w_inter * jnp.einsum("bthd,bhd->bth", qc, n)
        h = num / jnp.maximum(jnp.abs(den), jnp.exp(-mt))[..., None]
        tot = b[:, -1]
        g = tot[:, None, :] - b + ic
        m_new = jnp.maximum(tot + m, jnp.max(g, axis=1))
        decay = jnp.exp(tot + m - m_new)
        ws = jnp.exp(g - m_new[:, None, :])
        C_new = decay[..., None, None] * C + jnp.einsum("bsh,bshd,bshe->bhde", ws, kc, vc)
        n_new = decay[..., None] * n + jnp.einsum("bsh,bshd->bhd", ws, kc)
        return (C_new, n_new, m_new), h

    init = (C0.astype(jnp.float32), n0.astype(jnp.float32), m0.astype(jnp.float32))
    (C, n, m), h = lax.scan(step, init, xs)
    h = jnp.moveaxis(h, 0, 1).reshape(bsz, seq, N_LSTM_HEADS, LSTM_HEAD_DIM)
    return h, C, n, m

def _merge(att, h, mo, g_out, w_out):
    hl = _rmsnorm(jax.nn.sigmoid(mo) * h.astype(mo.dtype), g_out)
    lead = att.shape[:-1]
    mixed = jnp.concatenate([att.astype(hl.dtype), hl.reshape(lead + (LSTM_WIDTH,))], axis=-1)
    return mixed @ w_out

def _mix_prompt(x, rows, g_mix, w_in, b_i, b_f, g_q, g_k, sinks, g_out, w_out):
    bsz, seq = x.shape[:2]
    nb = seq // CHUNK
    q, k, v, mq, mk, mv, mo, li, lf = _in_proj(x, g_mix, w_in, b_i, b_f)
    q = _rmsnorm(q, g_q)
    k = _rmsnorm(k, g_k)

    def band(t):
        t = t.reshape(bsz, nb, CHUNK, N_KV_HEADS, HEAD_DIM)
        t = jnp.concatenate([jnp.zeros((bsz, WINDOW_CHUNKS) + t.shape[2:], t.dtype), t], axis=1)
        return jnp.concatenate([t[:, w:w + nb] for w in range(WINDOW_CHUNKS + 1)], axis=2)

    n_keys = (WINDOW_CHUNKS + 1) * CHUNK
    qi = jnp.arange(CHUNK)[:, None]
    kj = jnp.arange(n_keys)[None, :]
    dist = jnp.abs(WINDOW + qi - kj)
    valid = (jnp.arange(nb)[:, None] - WINDOW_CHUNKS) * CHUNK + kj >= 0
    att = _sink_attention(q.reshape(bsz, nb, CHUNK, N_KV_HEADS, GQA_GROUP, HEAD_DIM),
                          band(k), band(v), dist, valid, sinks)
    C0 = jnp.zeros((bsz, N_LSTM_HEADS, LSTM_HEAD_DIM, LSTM_HEAD_DIM), jnp.float32)
    n0 = jnp.zeros((bsz, N_LSTM_HEADS, LSTM_HEAD_DIM), jnp.float32)
    m0 = jnp.zeros((bsz, N_LSTM_HEADS), jnp.float32)
    h, C, n, m = _mlstm_scan(mq, mk, mv, li, lf, C0, n0, m0, CHUNK)
    y = _merge(att.reshape(bsz, seq, ATT_WIDTH), h, mo, g_out, w_out)
    return y, k[:, -rows:], v[:, -rows:], C, n, m

def _mix_sample(x, ck, cv, C0, n0, m0, g_mix, w_in, b_i, b_f, g_q, g_k, sinks, g_out, w_out):
    bsz, t = x.shape[:2]
    rows = ck.shape[1]
    q, k, v, mq, mk, mv, mo, li, lf = _in_proj(x, g_mix, w_in, b_i, b_f)
    q = _rmsnorm(q, g_q)
    k = _rmsnorm(k, g_k)
    kk = jnp.concatenate([ck.astype(k.dtype), k], axis=1)
    vv = jnp.concatenate([cv.astype(v.dtype), v], axis=1)
    dist = jnp.abs(rows + jnp.arange(t)[:, None] - jnp.arange(rows + t)[None, :])
    valid = jnp.ones((1, rows + t), dtype=bool)
    att = _sink_attention(q.reshape(bsz, 1, t, N_KV_HEADS, GQA_GROUP, HEAD_DIM),
                          kk[:, None], vv[:, None], dist, valid, sinks)
    h, C, n, m = _mlstm_scan(mq, mk, mv, li, lf, C0, n0, m0, t)
    y = _merge(att.reshape(bsz, t, ATT_WIDTH), h, mo, g_out, w_out)
    return y, kk[:, -rows:], vv[:, -rows:], C, n, m

def setup_inputs(seed: int = 0) -> dict:
    key = jax.random.key(seed)
    ks = jax.random.split(key, 32)
    f32 = jnp.float32
    rows = min(WINDOW, PAST_LEN)

    def nrm(k, shape, scale):
        return jax.random.normal(k, shape, f32) * scale

    def gain(k, shape):
        return 1.0 + 0.05 * jax.random.normal(k, shape, f32)

    return {
        "x_prompt": nrm(ks[0], (BATCH, SEQ, D_MODEL), 1.0),
        "x_sample": nrm(ks[1], (DEC_BATCH, DEC_SEQ, D_MODEL), 1.0),
        "cache_k": nrm(ks[2], (DEPTH, DEC_BATCH, rows, N_KV_HEADS, HEAD_DIM), 1.0),
        "cache_v": nrm(ks[3], (DEPTH, DEC_BATCH, rows, N_KV_HEADS, HEAD_DIM), 1.0),
        "state_C": nrm(ks[4], (DEPTH, DEC_BATCH, N_LSTM_HEADS, LSTM_HEAD_DIM, LSTM_HEAD_DIM), 0.3),
        "state_n": nrm(ks[5], (DEPTH, DEC_BATCH, N_LSTM_HEADS, LSTM_HEAD_DIM), 0.3),
        "state_m": jax.random.uniform(ks[6], (DEPTH, DEC_BATCH, N_LSTM_HEADS), f32, 0.0, 2.0),
        "g_ffn1": gain(ks[7], (DEPTH, D_MODEL)),
        "w1_gate": nrm(ks[8], (DEPTH, D_MODEL, D_FF), D_MODEL ** -0.5),
        "w1_up": nrm(ks[9], (DEPTH, D_MODEL, D_FF), D_MODEL ** -0.5),
        "w1_down": nrm(ks[10], (DEPTH, D_FF, D_MODEL), D_FF ** -0.5),
        "g_mix": gain(ks[11], (DEPTH, D_MODEL)),
        "w_in": nrm(ks[12], (DEPTH, D_MODEL, D_IN_PROJ), D_MODEL ** -0.5),
        "b_igate": nrm(ks[13], (DEPTH, N_LSTM_HEADS), 0.1),
        "b_fgate": jnp.broadcast_to(jnp.linspace(3.0, 6.0, N_LSTM_HEADS, dtype=f32), (DEPTH, N_LSTM_HEADS))
                   + nrm(ks[14], (DEPTH, N_LSTM_HEADS), 0.1),
        "g_q": gain(ks[15], (DEPTH, HEAD_DIM)),
        "g_k": gain(ks[16], (DEPTH, HEAD_DIM)),
        "attn_sinks": nrm(ks[17], (DEPTH, N_ATT_HEADS), 0.5),
        "g_lstm_out": gain(ks[18], (DEPTH, N_LSTM_HEADS, LSTM_HEAD_DIM)),
        "w_out": nrm(ks[19], (DEPTH, D_MIX, D_MODEL), D_MIX ** -0.5),
        "g_ffn2": gain(ks[20], (DEPTH, D_MODEL)),
        "w2_gate": nrm(ks[21], (DEPTH, D_MODEL, D_FF), D_MODEL ** -0.5),
        "w2_up": nrm(ks[22], (DEPTH, D_MODEL, D_FF), D_MODEL ** -0.5),
        "w2_down": nrm(ks[23], (DEPTH, D_FF, D_MODEL), D_FF ** -0.5),
        "g_final": gain(ks[24], (DEPTH, D_MODEL)),
    }

def reference(x_prompt, x_sample, cache_k, cache_v, state_C, state_n, state_m,
              g_ffn1, w1_gate, w1_up, w1_down, g_mix, w_in, b_igate, b_fgate,
              g_q, g_k, attn_sinks, g_lstm_out, w_out, g_ffn2, w2_gate, w2_up, w2_down, g_final):
    rows = cache_k.shape[2]
    xp, xs = x_prompt, x_sample
    kp_l, vp_l, Cp_l, np_l, mp_l = [], [], [], [], []
    ks_l, vs_l, Cs_l, ns_l, ms_l = [], [], [], [], []
    for l in range(DEPTH):
        mix_w = (g_mix[l], w_in[l], b_igate[l], b_fgate[l], g_q[l], g_k[l],
                 attn_sinks[l], g_lstm_out[l], w_out[l])
        xp = xp + _swiglu_half(xp, g_ffn1[l], w1_gate[l], w1_up[l], w1_down[l])
        dp, kp, vp, Cp, n_p, mp = _mix_prompt(xp, rows, *mix_w)
        xp = xp + dp
        xp = xp + _swiglu_half(xp, g_ffn2[l], w2_gate[l], w2_up[l], w2_down[l])
        xp = _rmsnorm(xp, g_final[l])
        xs = xs + _swiglu_half(xs, g_ffn1[l], w1_gate[l], w1_up[l], w1_down[l])
        ds, k_s, v_s, Cs, n_s, m_s = _mix_sample(xs, cache_k[l], cache_v[l], state_C[l],
                                                 state_n[l], state_m[l], *mix_w)
        xs = xs + ds
        xs = xs + _swiglu_half(xs, g_ffn2[l], w2_gate[l], w2_up[l], w2_down[l])
        xs = _rmsnorm(xs, g_final[l])
        kp_l.append(kp.astype(cache_k.dtype)); vp_l.append(vp.astype(cache_v.dtype))
        Cp_l.append(Cp.astype(state_C.dtype)); np_l.append(n_p.astype(state_n.dtype))
        mp_l.append(mp.astype(state_m.dtype))
        ks_l.append(k_s.astype(cache_k.dtype)); vs_l.append(v_s.astype(cache_v.dtype))
        Cs_l.append(Cs.astype(state_C.dtype)); ns_l.append(n_s.astype(state_n.dtype))
        ms_l.append(m_s.astype(state_m.dtype))
    k_prompt = jnp.stack(kp_l, 0)
    v_prompt = jnp.stack(vp_l, 0)
    C_prompt = jnp.stack(Cp_l, 0)
    n_prompt = jnp.stack(np_l, 0)
    m_prompt = jnp.stack(mp_l, 0)
    k_sample = jnp.stack(ks_l, 0)
    v_sample = jnp.stack(vs_l, 0)
    C_sample = jnp.stack(Cs_l, 0)
    n_sample = jnp.stack(ns_l, 0)
    m_sample = jnp.stack(ms_l, 0)
    return (xp, xs, k_prompt, v_prompt, C_prompt, n_prompt, m_prompt,
            k_sample, v_sample, C_sample, n_sample, m_sample)


_drawn_inputs = setup_inputs


def setup_inputs(seed=0):
    import zlib

    import numpy as np

    out = dict(_drawn_inputs(seed))
    spreads = {}
    factors = {'g_q': 8.0, 'attn_sinks': 64.0, 'g_ffn2': 3.554}
    for name, (base, spread) in spreads.items():
        noise = np.random.default_rng([zlib.crc32(name.encode()), seed]).standard_normal(out[name].shape)
        drawn = base * np.exp(spread * noise) if base else spread * noise
        out[name] = jnp.asarray(drawn.astype(out[name].dtype))
    for name, factor in factors.items():
        out[name] = (out[name] * factor).astype(out[name].dtype)
    return out
```

```python
import concourse.bass as bass
from concourse import mybir
from collections import namedtuple
from contextlib import ExitStack

F32 = mybir.dt.float32
F32R = mybir.dt.float32r
ACT = mybir.ActivationFunctionType
ALU = mybir.AluOpType
AX = mybir.AxisListType

P = 128
D = 1024
KT = D // P
SEQ, DEC = 1024, 64
T = SEQ + DEC
NB = SEQ // P
NTILE = [(0, 364), (364, 362), (726, 362)]
NW = 364
FF = 2816
PAIRS = FF // (2 * P)
HEADS, KV, HD = 8, 2, 64
LH, LD = 4, 128
EPS = 1e-6
MASKED = 1e30
BOUND = 1e18
Q0, K0, V0, M0 = 0, 512, 640, 768
G0 = M0 + 4 * LH * LD
UNITS = 23
OUT_UNITS = KT


def wait_done(engine, semaphore, count):
    if not isinstance(count, int) or count > 0:
        engine.wait_ge(semaphore, count)


def build(nc, a, o):
    with ExitStack() as ctx:
        ctx.enter_context(nc.allow_non_contiguous_dma(reason="gains, biases and states: a few small transfers"))
        base = (nc.sbuf_base + 63) // 64 * 64
        at = {}

        def place(name, shape, dtype, offset):
            return nc.alloc_sbuf_tensor_at(name, shape, dtype, offset=base + offset)

        def region(name, size):
            at[name] = at.get("end", 0)
            at["end"] = at[name] + size
            return at[name]

        def sem(name):
            return ctx.enter_context(nc.semaphore(name))

        rX = region("x", KT * T * 4)
        rHH = region("hh", KT * T * 4)
        rHL = region("hl", KT * T * 4)
        rA = region("a", 4 * T * 4)
        rWG = region("wg", 2 * 4 * 4096)
        rRAW = region("raw", 4 * 4096)
        rD = region("d", 3 * 8192)
        rT = region("t", 8 * NW * 4)
        rC = region("c", 0)
        assert base + rC < nc.sbuf_usable_end

        X = place("X", [P, KT, T], F32, rX)
        HH = place("HH", [P, KT, T], F32R, rHH)
        HL = place("HL", [P, KT, T], F32R, rHL)
        XIN = place("XIN", [P, NB + 1, D], F32, rHH)
        AH = place("AH", [P, 2, T], F32R, rA)
        AL = place("AL", [P, 2, T], F32R, rA + 2 * T * 4)
        ATT = place("ATT", [P, 4, T], F32, rA)
        WGH = place("WGH", [P, 4, KT, P], F32R, rWG)
        WGL = place("WGL", [P, 4, KT, P], F32R, rWG + 4 * 4096)
        RAWG = place("RAWG", [P, KT, 2 * P], F32, rRAW)
        RAWU = place("RAWU", [P, KT, 2 * P], F32, rRAW + 8192)
        RAW4 = place("RAW4", [P, 4, KT, P], F32, rRAW)
        WDH = place("WDH", [P, 2, D], F32R, rD)
        WDL = place("WDL", [P, 2, D], F32R, rD + 8192)
        RAWD = place("RAWD", [P, 2, D], F32, rD + 16384)
        SQ = [place("SQa", [P, 4, NW], F32, rD + 16384), place("SQb", [P, 4, NW], F32, rT + 4 * NW * 4)]
        RS = place("RS", [P, NW], F32, rD + 16384 + 4 * NW * 4)
        ST = place("ST", [P, 2, NW], F32, rT)
        AT = place("AT", [P, 2, NW], F32, rT + 2 * NW * 4)

        ZST = place("ZST", [P, 4, NW], F32, rT)
        R1, R2, R3, R4 = (place(f"R{i + 1}", [LH, T], F32, rA + i * T * 4) for i in range(4))
        R5, R6 = (place(f"R{i + 5}", [LH, T], F32, rD + 3 * 8192 - (2 - i) * T * 4) for i in range(2))
        VT = place("VT", [P, T], F32, rD)
        KTT = place("KTT", [P, T], F32, rD + T * 4)
        SQC = place("SQC", [P, NW], F32, rD + 2 * T * 4)
        RSC = place("RSC", [P, NW], F32, rD + 2 * T * 4 + 1472)
        assert 4 * T * 4 + 2 * 1472 <= 3 * 8192 and 2 * T * 4 + 2 * 1472 <= 2 * 8192
        VTOK = place("VTOK", [P, NB + 1, P], F32, rA)
        KTOK = place("KTOK", [P, 2, P], F32, rA + (NB + 1) * 512)

        QB = place("QB", [P, 2, 4, P], F32, rD)
        KW = place("KW", [P, 2, 2, 2 * P], F32, rD + 4096)
        VW = place("VW", [P, 2, 2, P], F32, rD + 8192)
        SP = place("SP", [P, 4, 2 * P], F32, rD + 10240)
        PT = place("PT", [P, 2, 4, P], F32, rD + 14336)
        CKV = place("CKV", [P, P], F32, rD + 18432)
        CKT = place("CKT", [P, P], F32, rD + 18944)
        ZB = place("ZB", [P, 2, 16, P], F32, rD)
        ASM = place("ASM", [P, LH, P], F32, rD + 16384)
        QWI = place("QWI", [P, LH, P], F32, rD + 18432)
        KWS = place("KWS", [P, LH, P], F32, rD + 20480)
        VM = place("VM", [P, LH, P], F32, rD + 22528)
        GB = place("GB", [P, 2, 12, P], F32, rA)
        CN = place("CN", [P, LH, 2 * P], F32, rA + 12288)
        N0C = place("N0C", [P, LH], F32, rA + 16384)
        EX = place("EX", [P, LH, P], F32, rT)
        WN = place("WN", [P, LH, P], F32, rT + 2048)
        SQM = place("SQM", [P, LH, P], F32, rT + 4096)
        DM = place("DM", [P, LH, P], F32, rT + 6144)
        RM = place("RM", [P, LH, P], F32, rT + 8192)
        YO = place("YO", [P, 4, D], F32, rHH)
        GF = place("GF", [P, D], F32, rD)
        JUNK = place("JUNK", [P, 4, 512], F32, rT)

        IDENT = place("IDENT", [P, P], F32, rC)
        ONES = place("ONES", [P, P], F32, rC + 512)
        BD = place("BD", [P, P], F32, rC + 1024)
        DT = place("DT", [P, 2 * P], F32, rC + 1536)
        DTI = place("DTI", [P, 2 * P], mybir.dt.int32, rD)
        DT0 = place("DT0", [P, 2 * P], F32, rC + 2560)
        MC = place("MC", [P, P], F32, rC + 3584)
        COLS = place("COLS", [P, (NB + 1) * 8], F32, rC + 4096)
        small_at = rC + 4096 + (NB + 1) * 32

        def small(name, shape, partitions=P):
            nonlocal small_at
            size = 4
            for x in shape:
                size *= x
            tile = place(name, [partitions, *shape], F32, small_at)
            small_at += (size + 31) // 32 * 32
            return tile

        GC = small("GC", [3, KT])
        GQ = small("GQ", [2])
        GO = small("GO", [LH])
        SINK = small("SINK", [HEADS])
        NSINK = small("NSINK", [HEADS])
        GATE = small("GATE", [4], LH)
        GBF = small("GBF", [1], 32 + LH)
        EPSC = small("EPSC", [1])
        NMX = small("NMX", [4])
        SUM = small("SUM", [4])
        ESK = small("ESK", [4])
        DEN = small("DEN", [4])
        FS = small("FS", [4, 4])
        assert base + small_at <= nc.sbuf_usable_end

        BANK = [ctx.enter_context(nc.psum_tensor(f"bank{i}", [P, 512], F32)) for i in range(8)]

        zqk = nc.dram_tensor("zqk", (5, P, T), F32, kind="Internal").ap()
        vtok = nc.dram_tensor("vtok", (NB + 1, P, P), F32, kind="Internal").ap()
        zm = nc.dram_tensor("zm", (4 * LH, P, T), F32, kind="Internal").ap()
        grow = nc.dram_tensor("grow", (3, LH, T), F32, kind="Internal").ap()

        const_in, const_ops, dist_abs = sem("const_in"), sem("const_ops"), sem("dist_abs")
        x_in = [sem(f"x_in{i}") for i in range(3)]
        x_tr, x_evA, x_evV = sem("x_tr"), sem("x_evA"), sem("x_evV")

        def named(prefix, names):
            return namedtuple(prefix, names)(*[sem(f"{prefix}_{n}") for n in names.split()])

        ffn = [named(f"f{i}", "gu_in d_in w_hi w_lo gu_mm d_mm silu mul a_hi a_ready x_add") for i in (1, 2)]
        norm = [named(f"n{i}", "sq ss rs rc ht hi lo") for i in range(3)]
        zin = [sem(f"z_in{s}") for s in range(4)]
        z = named("z", "padded hi lo mm ev sqc bd rsc zg rc scaled")
        zst = [sem(f"zst{s}") for s in range(4)]
        g = named("g", "i f ab e ln lf b m r u em w ws col colev out")
        vk = named("vk", "tr ev out kout cst cin ctr cev pad")
        at_in = [sem("at_in0"), sem("at_in1")]
        t_ = named("att", "s bias nmax nmin nmx ex den rden p tr ptA ptV o ev")
        m_in = [sem("m_in0"), sem("m_in1")]
        m_ = named("m", "d qw ex kvt kw v s asm num den upd cn w sq ss ad dm d2 v2 rs rc y hi lo c0 n0 cz cout")
        att_hi, att_lo, o_add = sem("att_hi"), sem("att_lo"), sem("o_add")
        fin = named("fin", "tr sq sum rs rc y g")
        fin_out = [sem(f"fin_out{i}") for i in range(4)]

        def x_view(k, n):
            t0, w = NTILE[n]
            return X[:, k, t0:t0 + w]

        def three_pass(bank, w, w_hi, w_lo, rhs_hi, rhs_lo, first, last):
            nc.tensor.matmul(bank[:, 0:w], w_hi, rhs_hi, start=first, stop=False)
            nc.tensor.matmul(bank[:, 0:w], w_hi, rhs_lo, start=False, stop=False)
            return nc.tensor.matmul(bank[:, 0:w], w_lo, rhs_hi, start=False, stop=last)

        def norm_act_root(act, s, n, bank):
            t0, w = NTILE[n]
            for h in range(2):
                if n:
                    act.wait_ge(s.lo, 2 * (n - 1) + h + 1)
                nc.scalar.activation(SQ[h][:, :, 0:w], X[:, 4 * h:4 * h + 4, t0:t0 + w], ACT.Square).then_inc(s.sq, 1)
            act.wait_ge(s.ss, n + 1)
            nc.scalar.activation(RS[:, 0:w], bank[:, 0:w], ACT.Sqrt, bias=EPSC[:, 0:1], scale=1.0 / D).then_inc(s.rs, 1)

        def norm_act_high(act, s, n):
            t0, w = NTILE[n]
            for h in range(2):
                act.wait_ge(s.ht, 2 * n + h + 1)
                nc.scalar.activation(HH[:, 4 * h:4 * h + 4, t0:t0 + w], SQ[h][:, :, 0:w], ACT.Copy).then_inc(s.hi, 1)

        def norm_pe(pe, s, n, bank):
            w = NTILE[n][1]
            if n:
                pe.wait_ge(s.rs, n)
            for k in range(KT):
                if k % 4 == 0:
                    pe.wait_ge(s.sq, 2 * n + k // 4 + 1)
                mm = nc.tensor.matmul(bank[:, 0:w], ONES[:, :], SQ[k // 4][:, k % 4, 0:w], start=(k == 0), stop=(k == KT - 1))
            mm.then_inc(s.ss, 1)

        def norm_dve(dve, s, n, which):
            w = NTILE[n][1]
            dve.wait_ge(s.rs, n + 1)
            nc.vector.reciprocal(RS[:, 0:w], RS[:, 0:w]).then_inc(s.rc, 1)
            dve.wait_ge(s.rc, n + 1)
            for k in range(KT):
                ht = nc.vector.scalar_tensor_tensor(out=SQ[k // 4][:, k % 4, 0:w], in0=x_view(k, n), scalar=GC[:, which, k:k + 1],
                                                    in1=RS[:, 0:w], op0=ALU.mult, op1=ALU.mult)
                if k % 4 == 3:
                    ht.then_inc(s.ht, 1)

        def norm_pool(pool, s, n):
            t0, w = NTILE[n]
            for h in range(2):
                pool.wait_ge(s.hi, 2 * n + h + 1)
                nc.gpsimd.tensor_tensor(HL[:, 4 * h:4 * h + 4, t0:t0 + w], SQ[h][:, :, 0:w],
                                        HH[:, 4 * h:4 * h + 4, t0:t0 + w].bitcast(F32), ALU.subtract).then_inc(s.lo, 1)

        def ffn_sp(sp, s, w_gate, w_up, w_down, before_gu, before_d):
            def gu(col):
                for raw, w in ((RAWG, w_gate), (RAWU, w_up)):
                    sp.dma_start(raw[:, :, :], w[:, bass.ds(col, 2 * P)].rearrange("(k p) c -> p k c", p=P)).then_inc(s.gu_in, 16)

            def down(row):
                sp.dma_start(RAWD[:, :, :], w_down[bass.ds(row, 2 * P), :].rearrange("(k p) c -> p k c", p=P)).then_inc(s.d_in, 16)

            before_gu()
            gu(0)
            before_d()
            down(0)
            with sp.Fori(1, PAIRS) as p:
                sp.wait_ge(s.w_lo, p * 6 - 2)
                gu(p * (2 * P))
                sp.wait_ge(s.w_lo, p * 6)
                down(p * (2 * P))

        def raw_gu(c):
            raw = RAWU if c % 2 else RAWG
            return raw[:, :, (c // 2) * P:(c // 2 + 1) * P]

        def ffn_act_gu_high(act, s, p, c, first=False):
            act.wait_ge(s.gu_in, p * 32 + 32)
            if not first:
                act.wait_ge(s.gu_mm, p * 12 - 4 + c + 1)
            nc.scalar.activation(WGH[:, c], raw_gu(c), ACT.Copy).then_inc(s.w_hi, 1)

        def ffn_dve_gu_low(dve, s, p, c):
            dve.wait_ge(s.w_hi, p * 6 + c + 1)
            nc.vector.tensor_tensor(WGL[:, c], raw_gu(c), WGH[:, c].bitcast(F32), ALU.subtract).then_inc(s.w_lo, 1)

        def ffn_act_down_high(act, s, p, d, first=False):
            act.wait_ge(s.d_in, p * 16 + 16)
            if not first:
                act.wait_ge(s.d_mm, p * 24)
            nc.scalar.activation(WDH[:, d], RAWD[:, d], ACT.Copy).then_inc(s.w_hi, 1)

        def ffn_dve_down_low(dve, s, p, d):
            dve.wait_ge(s.w_hi, p * 6 + 4 + d + 1)
            nc.vector.tensor_tensor(WDL[:, d], RAWD[:, d], WDH[:, d].bitcast(F32), ALU.subtract).then_inc(s.w_lo, 1)

        def ffn_pe_gu(pe, s, p, n, c, first=False):
            t0, w = NTILE[n]
            t = c // 2
            pe.wait_ge(s.w_lo, p * 6 + c + 1)
            if not (first and n == 0):
                pe.wait_ge(s.mul if c % 2 else s.silu, p * 6 + 2 * n + t - 1)
            for k in range(KT):
                mm = three_pass(BANK[4 + c], w, WGH[:, c, k], WGL[:, c, k], HH[:, k, t0:t0 + w], HL[:, k, t0:t0 + w], k == 0, k == KT - 1)
            mm.then_inc(s.gu_mm, 1)

        def ffn_pe_down(pe, s, p, n):
            t0, w = NTILE[n]
            pe.wait_ge(s.a_ready, p * 6 + 2 * n + 2)
            if n == 0:
                pe.wait_ge(s.w_lo, p * 6 + 6)
            for m in range(KT):
                if n or m >= 4:
                    pe.wait_ge(s.x_add, p * 24 + 8 * n + m - 3)
                for d in range(2):
                    c = slice(m * P, m * P + P)
                    mm = three_pass(BANK[m % 4], w, WDH[:, d, c], WDL[:, d, c], AH[:, d, t0:t0 + w], AL[:, d, t0:t0 + w], d == 0, d == 1)
                mm.then_inc(s.d_mm, 1)

        def ffn_act_silu(act, s, p, n, t, first=False):
            w = NTILE[n][1]
            act.wait_ge(s.gu_mm, p * 12 + 4 * n + 2 * t + 1)
            if not (first and n == 0):
                act.wait_ge(s.mul, p * 6 + 2 * n + t - 1)
            nc.scalar.activation(ST[:, t, 0:w], BANK[4 + 2 * t][:, 0:w], ACT.Silu).then_inc(s.silu, 1)

        def ffn_dve_a(dve, s, p, n, t, first=False):
            t0, w = NTILE[n]
            dve.wait_ge(s.silu, p * 6 + 2 * n + t + 1)
            dve.wait_ge(s.gu_mm, p * 12 + 4 * n + 2 * t + 2)
            nc.vector.tensor_tensor(AT[:, t, 0:w], ST[:, t, 0:w], BANK[5 + 2 * t][:, 0:w], ALU.mult).then_inc(s.mul, 1)
            dve.wait_ge(s.mul, p * 6 + 2 * n + t + 1)
            if not first:
                dve.wait_ge(s.d_mm, p * 24 - 24 + 8 * n + 8)
            nc.vector.tensor_copy(AH[:, t, t0:t0 + w], AT[:, t, 0:w]).then_inc(s.a_hi, 1)
            dve.wait_ge(s.a_hi, p * 6 + 2 * n + t + 1)
            nc.vector.tensor_tensor(AL[:, t, t0:t0 + w], AT[:, t, 0:w], AH[:, t, t0:t0 + w].bitcast(F32), ALU.subtract).then_inc(s.a_ready, 1)

        def ffn_dve_x(dve, s, p, n):
            w = NTILE[n][1]
            for m in range(KT):
                dve.wait_ge(s.d_mm, p * 24 + 8 * n + m + 1)
                nc.vector.scalar_tensor_tensor(out=x_view(m, n), in0=BANK[m % 4][:, 0:w], scalar=0.5, in1=x_view(m, n),
                                               op0=ALU.mult, op1=ALU.add).then_inc(s.x_add, 1)

        def ffn_act(act, s, ns):
            for n in range(3):
                if n < 2:
                    norm_act_root(act, ns, n + 1, BANK[0])
                if n == 2:
                    for d in range(2):
                        ffn_act_down_high(act, s, 0, d, first=True)
                for t in range(2):
                    ffn_act_silu(act, s, 0, n, t, first=True)
                    if n == 2:
                        ffn_act_gu_high(act, s, 1, 2 * t)
                        ffn_act_gu_high(act, s, 1, 2 * t + 1)
                if n < 2:
                    norm_act_high(act, ns, n + 1)

            def body(p, last):
                for n in range(3):
                    if n == 2:
                        for d in range(2):
                            ffn_act_down_high(act, s, p, d)
                    for t in range(2):
                        ffn_act_silu(act, s, p, n, t)
                        if n == 2 and not last:
                            ffn_act_gu_high(act, s, p + 1, 2 * t)
                            ffn_act_gu_high(act, s, p + 1, 2 * t + 1)
            with act.Fori(1, PAIRS - 1) as p:
                body(p, False)
            body(PAIRS - 1, True)

        def ffn_dve(dve, s, ns, which):
            for n in range(3):
                if n < 2:
                    norm_dve(dve, ns, n + 1, which)
                if n == 2:
                    for d in range(2):
                        ffn_dve_down_low(dve, s, 0, d)
                for t in range(2):
                    ffn_dve_a(dve, s, 0, n, t, first=True)
                    if n == 2:
                        ffn_dve_gu_low(dve, s, 1, 2 * t)
                        ffn_dve_gu_low(dve, s, 1, 2 * t + 1)

            def body(p, last):
                for n in range(3):
                    ffn_dve_x(dve, s, p - 1, n)
                    if n == 2:
                        for d in range(2):
                            ffn_dve_down_low(dve, s, p, d)
                    for t in range(2):
                        ffn_dve_a(dve, s, p, n, t)
                        if n == 2 and not last:
                            ffn_dve_gu_low(dve, s, p + 1, 2 * t)
                            ffn_dve_gu_low(dve, s, p + 1, 2 * t + 1)
            with dve.Fori(1, PAIRS - 1) as p:
                body(p, False)
            body(PAIRS - 1, True)

        def ffn_pe(pe, s, ns):
            for n in range(3):
                pe.wait_ge(ns.lo, 2 * n + 2)
                for c in range(4):
                    ffn_pe_gu(pe, s, 0, n, c, first=True)
                    if c == 0 and n < 2:
                        norm_pe(pe, ns, n + 1, BANK[0])
            with pe.Fori(1, PAIRS) as p:
                for n in range(3):
                    ffn_pe_down(pe, s, p - 1, n)
                    for c in range(4):
                        ffn_pe_gu(pe, s, p, n, c)

        LAST = PAIRS - 1

        def unit_high(act, slot, loads, freed=None):
            if freed is not None:
                act.wait_ge(z.mm, freed)
            act.wait_ge(zin[slot], loads * 16)
            nc.scalar.activation(WGH[:, slot], RAW4[:, slot], ACT.Copy).then_inc(z.hi, 1)

        def unit_low(dve, j, slot):
            dve.wait_ge(z.hi, j)
            nc.vector.tensor_tensor(WGL[:, slot], RAW4[:, slot], WGH[:, slot].bitcast(F32), ALU.subtract).then_inc(z.lo, 1)

        def loads_until(j):
            return (j - 4) // 4 + 1 if j % 4 == 0 else (j - j % 4) // 4 + 1 + (j % 4 == 1)

        def unit_chain(pe, n, slot, bank):
            t0, w = NTILE[n]
            for k in range(KT):
                mm = three_pass(bank, w, WGH[:, slot, k], WGL[:, slot, k], HH[:, k, t0:t0 + w], HL[:, k, t0:t0 + w], k == 0, k == KT - 1)
            mm.then_inc(z.mm, 1)

        M1 = [(j, n) for n in range(3) for j in (1, 2, 3, 4)] + [(j, n) for j in (5, 6, 7) for n in range(3)]
        PLAIN = [c for c, (j, n) in enumerate(M1) if j < 3]
        NORMED = [c for c, (j, n) in enumerate(M1) if j >= 3]
        STORED = [c for c, (j, n) in enumerate(M1) if j >= 4]
        C1 = len(M1)
        E1 = len(PLAIN)
        HEAD_ORDER = (0, 2, 1, 3)

        block = ctx.enter_context(nc.Block())

        @block.sync
        def _(sp):
            sp.dma_start(XIN[:, 0:4, :], a["x_prompt"][0, 0:512, :].rearrange("(b p) f -> p b f", p=P)).then_inc(x_in[0], 16)
            sp.dma_start(XIN[:, 4:8, :], a["x_prompt"][0, 512:1024, :].rearrange("(b p) f -> p b f", p=P)).then_inc(x_in[1], 16)
            sp.dma_start(XIN[0:DEC, 8, :], a["x_sample"][0, :, :]).then_inc(x_in[2], 16)

            ffn_sp(sp, ffn[0], a["w1_gate"][0], a["w1_up"][0], a["w1_down"][0],
                   lambda: None, lambda: sp.wait_ge(norm[0].lo, 6))

            w_in, w_out = a["w_in"][0], a["w_out"][0]
            sp.wait_ge(ffn[0].w_lo, 6 * PAIRS - 2)
            sp.wait_ge(z.padded, 1)
            for gate in range(2):
                col = G0 + gate * LH
                sp.dma_start(RAW4[:, 1, :, 32 * gate:32 * gate + LH], w_in[:, col:col + LH].rearrange("(k p) c -> p k c", p=P)).then_inc(zin[1], 16)

            def load(slot, w, col):
                sp.dma_start(RAW4[:, slot], w[:, bass.ds(col, P)].rearrange("(k p) c -> p k c", p=P)).then_inc(zin[slot], 16)

            for j, col in ((2, V0), (3, K0), (4, Q0)):
                load(j % 4, w_in, col)
            for j in (5, 6, 7):
                sp.wait_ge(z.lo, j - 4)
                load(j % 4, w_in, Q0 + (j - 4) * P)
            with sp.Fori(0, LH) as h:
                for t in range(4):
                    sp.wait_ge(z.lo, h * 4 + (t + 4))
                    load(t, w_in, h * P + (M0 + t * LH * P))
            with sp.Fori(0, 2) as i:
                for t in range(4):
                    sp.wait_ge(z.lo, i * 4 + (t + UNITS - 3))
                    load(t, w_out, i * (4 * P) + t * P)

            ffn_sp(sp, ffn[1], a["w2_gate"][0], a["w2_up"][0], a["w2_down"][0],
                   lambda: sp.wait_ge(z.lo, UNITS + OUT_UNITS), lambda: sp.wait_ge(norm[2].lo, 6))

            for b in range(NB + 1):
                sp.wait_ge(fin.y, 2 * b + 2)
                if b < NB:
                    sp.dma_start(o[0][0, b * P:(b + 1) * P, :], YO[:, b % 4, :]).then_inc(fin_out[b % 4], 16)
                else:
                    sp.dma_start(o[1][0, :, :], YO[0:DEC, b % 4, :]).then_inc(fin_out[b % 4], 16)
            for i in range(4):
                sp.wait_ge(fin_out[i], 16 * ((NB - i) // 4 + 1))

        @block.gpsimd
        def _(pool):
            def const(dst, src):
                pool.dma_start(dst, src).then_inc(const_in, 16)
            for i, name in enumerate(("g_ffn1", "g_mix", "g_ffn2")):
                const(GC[:, i, :], a[name][0].rearrange("(k p) -> p k", p=P))
            for c, name in enumerate(("g_q", "g_k")):
                for half in range(2):
                    const(GQ[half * HD:(half + 1) * HD, c:c + 1], a[name].rearrange("o p -> p o"))
            const(GO[:, :], a["g_lstm_out"][0].rearrange("h p -> p h"))
            const(SINK[:, :], a["attn_sinks"][0].partition_broadcast(P))
            const(GATE[:, 0:1], a["b_igate"].rearrange("o p -> p o"))
            const(GBF[32:32 + LH, 0:1], a["b_fgate"].rearrange("o p -> p o"))
            const(GATE[:, 2:3], a["state_m"][0].rearrange("o p -> p o"))

            nc.gpsimd.memset(IDENT[:, :], 0.0).then_inc(const_ops, 1)
            nc.gpsimd.memset(ONES[:, :], 1.0).then_inc(const_ops, 1)
            nc.gpsimd.memset(BD[:, :], 0.0).then_inc(const_ops, 1)
            nc.gpsimd.memset(MC[:, :], 0.0).then_inc(const_ops, 1)
            nc.gpsimd.memset(EPSC[:, :], EPS).then_inc(const_ops, 1)
            nc.gpsimd.iota(DTI[:, :], [[-1, 2 * P]], base=P, channel_multiplier=1).then_inc(const_ops, 1)
            pool.wait_ge(const_ops, 6)
            nc.gpsimd.affine_select(out=IDENT[:, :], in_=IDENT[:, :], compare_op=ALU.not_equal, fill=1.0, base=0,
                                    pattern=[[-1, P]], channel_multiplier=1).then_inc(const_ops, 1)
            nc.gpsimd.affine_select(out=MC[:, :], in_=MC[:, :], compare_op=ALU.is_ge, fill=-MASKED, base=0,
                                    pattern=[[1, P]], channel_multiplier=-1).then_inc(const_ops, 1)
            pool.wait_ge(const_ops, 8)
            nc.gpsimd.memset(GATE[:, 1:2], 0.0).then_inc(const_ops, 1)
            pool.wait_ge(const_ops, 9)
            nc.gpsimd.memset(BD[0:HD, 0:HD], 1.0).then_inc(const_ops, 1)
            pool.wait_ge(const_ops, 10)
            nc.gpsimd.memset(BD[HD:P, HD:P], 1.0).then_inc(const_ops, 1)
            pool.wait_ge(const_ops, 11)
            pool.wait_ge(dist_abs, 1)
            nc.gpsimd.memset(DT[0:HD, 3 * HD:4 * HD], MASKED).then_inc(const_ops, 1)
            pool.wait_ge(const_ops, 12)
            nc.gpsimd.memset(DT[HD:P, 0:HD], MASKED).then_inc(const_ops, 1)
            pool.wait_ge(const_ops, 13)
            nc.gpsimd.tensor_copy(DT0[:, P:2 * P], DT[:, P:2 * P]).then_inc(const_ops, 1)
            nc.gpsimd.memset(DT0[:, 0:P], MASKED).then_inc(const_ops, 1)

            for n in range(3):
                norm_pool(pool, norm[0], n)
            pool.dma_start(o[7][0, 0, 0:HD], a["cache_k"][0, 0, HD:P]).then_inc(vk.cst, 16)
            pool.dma_start(o[8][0, 0, 0:HD], a["cache_v"][0, 0, HD:P]).then_inc(vk.cst, 16)
            pool.wait_ge(ffn[0].w_lo, 6 * PAIRS - 2)
            nc.gpsimd.memset(RAW4[:, 1, :, :], 0.0).then_inc(z.padded, 1)

            for n in range(3):
                norm_pool(pool, norm[1], n)

            for q, c in enumerate(STORED):
                j, n = M1[c]
                t0, w = NTILE[n]
                pool.wait_ge(z.scaled, NORMED.index(c) + 1)
                pool.dma_start(zqk[j - 3, :, t0:t0 + w], ZST[:, q % 4, 0:w]).then_inc(zst[q % 4], 16)
                if q == 2:
                    pool.dma_start(zqk[0, :, :], KTT[:, :]).then_inc(vk.kout, 16)
            pool.wait_ge(g.ws, NB + 1)
            pool.wait_ge(g.w, NB + 1)
            for i, r in enumerate((R3, R5, R2)):
                pool.dma_start(grow[i], r[:, :]).then_inc(g.out, 16)
            pool.dma_start(o[6].rearrange("o b h -> h (o b)"), R4[:, SEQ - 1:SEQ]).then_inc(g.out, 16)
            pool.dma_start(o[11].rearrange("o b h -> h (o b)"), R4[:, T - 1:T]).then_inc(g.out, 16)
            pool.wait_ge(vk.ev, 3)
            flat = lambda ap: ap.rearrange("p h d -> p (h d)")
            pool.dma_start(vtok[0:NB].rearrange("b p f -> p b f"), VTOK[:, 0:NB, :]).then_inc(vk.out, 16)
            pool.dma_start(vtok[NB, 0:DEC], VTOK[0:DEC, NB, :]).then_inc(vk.out, 16)
            pool.dma_start(flat(o[3][0, 0]), VTOK[:, NB - 1, :]).then_inc(vk.out, 16)
            pool.dma_start(flat(o[8][0, 0, HD:P]), VTOK[0:DEC, NB, :]).then_inc(vk.out, 16)
            pool.dma_start(flat(o[2][0, 0]), KTOK[:, 0, :]).then_inc(vk.out, 16)
            pool.dma_start(flat(o[7][0, 0, HD:P]), KTOK[0:DEC, 1, :]).then_inc(vk.out, 16)
            for q in range(4):
                pool.wait_ge(zst[q], 16 * 3)
            pool.wait_ge(vk.kout, 16)
            pool.wait_ge(vk.out, 16 * 6)
            pool.wait_ge(g.out, 16 * 5)

            def att_load(par, q_col, k_col, v_block):
                s = at_in[par]
                pool.dma_start(QB[:, par], zqk[1:5, :, bass.ds(q_col, P)].rearrange("t p c -> p t c")).then_inc(s, 16)
                pool.dma_start(KW[:, par, 0], zqk[0, :, bass.ds(k_col, 2 * P)]).then_inc(s, 16)
                for g_ in range(2):
                    pool.dma_start(KW[g_ * HD:(g_ + 1) * HD, par, 1], zqk[0, (1 - g_) * HD:(2 - g_) * HD, bass.ds(k_col, 2 * P)]).then_inc(s, 16)
                pool.dma_start(VW[:, par], vtok[bass.ds(v_block, 2)].rearrange("b p f -> p b f")).then_inc(s, 16)

            pool.dma_start(QB[:, 0], zqk[1:5, :, 0:P].rearrange("t p c -> p t c")).then_inc(at_in[0], 16)
            for w in range(2):
                wc = slice(w * P, (w + 1) * P)
                pool.dma_start(KW[:, 0, 0, wc], zqk[0, :, 0:P]).then_inc(at_in[0], 16)
                for g_ in range(2):
                    pool.dma_start(KW[g_ * HD:(g_ + 1) * HD, 0, 1, wc], zqk[0, (1 - g_) * HD:(2 - g_) * HD, 0:P]).then_inc(at_in[0], 16)
                pool.dma_start(VW[:, 0, w], vtok[0]).then_inc(at_in[0], 16)
            att_load(1, P, 0, 0)

            def stores(h, t):
                for n in range(3):
                    t0, w = NTILE[n]
                    pool.wait_ge(z.ev, h * 12 + (E1 + 3 * t + n + 1))
                    pool.dma_start(zm[bass.ds(h + t * LH, 1), :, t0:t0 + w].rearrange("o p c -> (o p) c"),
                                   ZST[:, (3 * t + n) % 4, 0:w]).then_inc(zst[(3 * t + n) % 4], 16)

            with pool.Fori(0, LH - 1) as h:
                for t in range(4):
                    stores(h, t)
                    if t % 2:
                        pool.wait_ge(t_.ev, h * 4 + (t + 1))
                        i = t // 2
                        att_load(i, h * (2 * P) + (2 + i) * P, h * (2 * P) + (1 + i) * P, h * 2 + (1 + i))
            for t in range(2):
                stores(LH - 1, t)
            pool.wait_ge(t_.ev, 4 * (LH - 1) + 2)
            nc.gpsimd.memset(QB[:, 0, :, DEC:P], 0.0).then_inc(vk.pad, 1)
            nc.gpsimd.memset(KW[:, 0, :, P + DEC:2 * P], 0.0).then_inc(vk.pad, 1)
            pool.wait_ge(vk.pad, 2)
            nc.gpsimd.memset(VW[DEC:P, 0, 1, :], 0.0).then_inc(vk.pad, 1)
            pool.wait_ge(vk.pad, 3)
            pool.dma_start(QB[:, 0, :, 0:DEC], zqk[1:5, :, SEQ:T].rearrange("t p c -> p t c")).then_inc(at_in[0], 16)
            pool.dma_start(KW[:, 0, 0, P:P + DEC], zqk[0, :, SEQ:T]).then_inc(at_in[0], 16)
            for g_ in range(2):
                pool.dma_start(KW[g_ * HD:(g_ + 1) * HD, 0, 1, P:P + DEC], zqk[0, (1 - g_) * HD:(2 - g_) * HD, SEQ:T]).then_inc(at_in[0], 16)
            pool.dma_start(VW[0:DEC, 0, 1, :], vtok[NB, 0:DEC]).then_inc(at_in[0], 16)
            pool.dma_start(VW[:, 0, 0, :], flat(a["cache_v"][0, 0])).then_inc(at_in[0], 16)
            pool.dma_start(CKV[:, :], flat(a["cache_k"][0, 0])).then_inc(vk.cin, 16)
            for t in range(2, 4):
                stores(LH - 1, t)
            pool.wait_ge(vk.cev, 1)
            pool.dma_start(KW[:, 0, 0, 0:P], CKT[:, :]).then_inc(at_in[0], 16)
            for g_ in range(2):
                pool.dma_start(KW[g_ * HD:(g_ + 1) * HD, 0, 1, 0:P], CKT[(1 - g_) * HD:(2 - g_) * HD, :]).then_inc(at_in[0], 16)

            for q in range(4):
                pool.wait_ge(zst[q], 16 * (3 + 12))
            pool.wait_ge(t_.ev, 2 * (NB + 1))
            pool.wait_ge(att_lo, 1)

            def m_load(par, col, width=P):
                s = m_in[par]
                pool.dma_start(ZB[:, par, :, 0:width], zm[:, :, bass.ds(col, width)].rearrange("t p c -> p t c")).then_inc(s, 16)
                src = grow.rearrange("i h c -> (i h) c")[:, bass.ds(col, width)].partition_broadcast(P)
                pool.dma_start(GB[:, par, :, 0:width], src).then_inc(s, 16)

            def m_exponents(b, par, L, loads):
                pool.wait_ge(m_in[par], loads)
                wait_done(pool, m_.asm, b)
                nc.gpsimd.tensor_tensor(EX[0:L, :, 0:L], GB[0:L, par, 0:4, 0:L], MC[0:L, None, 0:L].broadcast_to([L, LH, L]), ALU.add).then_inc(m_.d, 1)
                wait_done(pool, m_.den, b)
                nc.gpsimd.tensor_tensor(QWI[:, :, 0:L], ZB[:, par, 0:4, 0:L], GB[:, par, 4:8, 0:L], ALU.mult).then_inc(m_.qw, 1)

            def m_low(b, L, col):
                pool.wait_ge(m_.hi, b + 1)
                nc.gpsimd.tensor_tensor(HL[:, 4:8, bass.ds(col, L)], WN[:, :, 0:L], HH[:, 4:8, bass.ds(col, L)].bitcast(F32), ALU.subtract).then_inc(m_.lo, 1)

            nc.gpsimd.memset(CN[:, :, :], 0.0).then_inc(m_.cz, 1)
            m_load(0, 0)
            m_load(1, P)
            m_exponents(0, 0, P, 32)

            def m_step(i, par, load_next, next_l=P):
                b = i * 2 + par
                pool.wait_ge(m_.cn, b + 1)
                if load_next:
                    load_next()
                nb_ = (i * 2 + par + 1)
                m_exponents(nb_, 1 - par, next_l, i * 32 + (32 if par == 0 else 64))
                m_low(b, P, i * (2 * P) + par * P)

            with pool.Fori(0, NB // 2 - 1) as i:
                for par in range(2):
                    m_step(i, par, lambda: m_load(par, i * (2 * P) + (2 + par) * P))
            m_step(NB // 2 - 1, 0, lambda: m_load(0, SEQ, DEC))
            pool.wait_ge(m_.cn, NB)
            pool.dma_start(o[4][0, 0].rearrange("h d e -> d h e"), CN[:, :, 0:P]).then_inc(m_.cout, 16)
            pool.dma_start(o[5][0, 0].rearrange("h d -> d h"), CN[:, :, P]).then_inc(m_.cout, 16)
            pool.dma_start(N0C[:, :], a["state_n"][0, 0].rearrange("h d -> d h")).then_inc(m_.c0, 16)
            pool.wait_ge(m_.cout, 32)
            pool.dma_start(CN[:, :, 0:P], a["state_C"][0, 0].rearrange("h d e -> d h e")).then_inc(m_.c0, 16)
            m_step(NB // 2 - 1, 1, None, DEC)
            pool.wait_ge(m_.cn, NB + 1)
            m_low(NB, DEC, SEQ)
            pool.dma_start(o[9][0, 0].rearrange("h d e -> d h e"), CN[:, :, 0:P]).then_inc(m_.cout, 16)
            pool.dma_start(o[10][0, 0].rearrange("h d -> d h"), CN[:, :, P]).then_inc(m_.cout, 16)
            pool.wait_ge(m_.cout, 64)
            pool.wait_ge(vk.cst, 32)

            for n in range(3):
                norm_pool(pool, norm[2], n)
            pool.wait_ge(ffn[1].d_mm, 24 * PAIRS)
            pool.dma_start(GF[:, :], a["g_final"][0].partition_broadcast(P)).then_inc(fin.g, 16)

        @block.scalar
        def _(act):
            act.wait_ge(const_ops, 6)
            nc.scalar.activation(DT[:, :], DTI[:, :], ACT.Abs).then_inc(dist_abs, 1)
            for b in range(NB + 1):
                L = P if b < NB else DEC
                act.wait_ge(x_tr, 2 * b + 1)
                nc.scalar.activation(X[:, 0:4, b * P:b * P + L], BANK[(2 * b) % 8][:, :].rearrange("p (k c) -> p k c", k=4)[:, :, 0:L], ACT.Copy).then_inc(x_evA, 1)
            act.wait_ge(x_evV, NB + 1)
            act.wait_ge(x_evA, NB + 1)
            act.wait_ge(const_ops, 15)
            norm_act_root(act, norm[0], 0, BANK[4])
            for c in range(4):
                ffn_act_gu_high(act, ffn[0], 0, c, first=True)
            norm_act_high(act, norm[0], 0)
            ffn_act(act, ffn[0], norm[0])

            act.wait_ge(ffn[0].x_add, 24 * LAST + 8)
            norm_act_root(act, norm[1], 0, BANK[4])
            norm_act_high(act, norm[1], 0)
            for j in (1, 2, 3, 4):
                unit_high(act, j % 4, loads_until(j))
            act.wait_ge(const_in, 16 * 12)
            act.wait_ge(ffn[0].x_add, 24 * PAIRS)

            plain = normed = 0
            for c, (j, n) in enumerate(M1):
                t0, w = NTILE[n]
                bank = BANK[c % 4]
                if c in (0, 4):
                    norm_act_root(act, norm[1], 1 + c // 4, BANK[4])
                act.wait_ge(z.mm, c + 1)
                if j == 1:
                    nc.scalar.activation(R1[:, t0:t0 + w], bank[0:LH, 0:w], ACT.Identity, bias=GATE[:, 0:1]).then_inc(g.i, 1)
                    nc.scalar.activation(R2[:, t0:t0 + w], bank[32:32 + LH, 0:w], ACT.Identity, bias=GBF[32:32 + LH, 0:1]).then_inc(z.ev, 1)
                    plain += 1
                elif j == 2:
                    nc.scalar.activation(VT[:, t0:t0 + w], bank[:, 0:w], ACT.Copy).then_inc(z.ev, 1)
                    plain += 1
                else:
                    nc.scalar.activation(SQC[:, 0:w], bank[:, 0:w], ACT.Square).then_inc(z.sqc, 1)
                    normed += 1
                    act.wait_ge(z.bd, normed)
                    if normed > 1:
                        act.wait_ge(z.scaled, normed - 1)
                    nc.scalar.activation(RSC[:, 0:w], BANK[5][:, 0:w], ACT.Sqrt, bias=EPSC[:, 0:1], scale=1.0 / HD).then_inc(z.rsc, 1)
                if n == 2:
                    unit_high(act, j % 4, loads_until(j + 4), freed=c + 1)
                if c in (2, 6):
                    norm_act_high(act, norm[1], 1 + c // 4)
                if c == 12:
                    act.wait_ge(z.ev, E1)
                    nc.scalar.activation(R3[:, :], R2[:, :], ACT.Abs).then_inc(g.ab, 1)
                    act.wait_ge(g.ab, 1)
                    nc.scalar.activation(R3[:, :], R3[:, :], ACT.Exp, scale=-1.0).then_inc(g.e, 1)
                    act.wait_ge(g.e, 1)
                    nc.scalar.activation(R3[:, :], R3[:, :], ACT.Ln, bias=1.0).then_inc(g.ln, 1)
                if c == 16:
                    act.wait_ge(g.u, 1)
                    nc.scalar.activation(R2[:, :], R4[:, :], ACT.Exp, scale=-1.0).then_inc(g.em, 1)
                    for b in range(NB + 1):
                        s0, s1 = b * P, min(b * P + P, T)
                        before = GATE[:, 1:2] if b == 0 else GATE[:, 2:3] if b == NB else R4[:, s0 - 1:s0]
                        nc.scalar.activation(R5[:, s0:s1], R3[:, s0:s1], ACT.Exp, bias=before).then_inc(g.w, 1)
                        nc.scalar.activation(R6[:, s0:s1], R1[:, s0:s1], ACT.Exp, bias=R3[:, s1 - 1:s1]).then_inc(g.ws, 1)
            act.wait_ge(g.col, 1)
            nc.scalar.activation(COLS[:, 0:8 * NB], BANK[6][:, 0:8 * NB], ACT.Copy).then_inc(g.colev, 1)
            nc.scalar.activation(COLS[0:DEC, 8 * NB:8 * NB + 8], BANK[6][0:DEC, 8 * NB:8 * NB + 8], ACT.Copy).then_inc(g.colev, 1)
            act.wait_ge(g.out, 16 * 5)
            act.wait_ge(vk.tr, 3)
            nc.scalar.activation(VTOK[:, 0:4, :], BANK[7][:, :].rearrange("p (b c) -> p b c", b=4), ACT.Copy).then_inc(vk.ev, 1)
            nc.scalar.activation(VTOK[:, 4:8, :], BANK[4][:, :].rearrange("p (b c) -> p b c", b=4), ACT.Copy).then_inc(vk.ev, 1)
            nc.scalar.activation(VTOK[0:DEC, NB, :], BANK[5][0:DEC, 0:P], ACT.Copy)
            nc.scalar.activation(KTOK[:, 0, :], BANK[5][:, P:2 * P], ACT.Copy)
            nc.scalar.activation(KTOK[0:DEC, 1, :], BANK[5][0:DEC, 2 * P:3 * P], ACT.Copy).then_inc(vk.ev, 1)

            def att_exps(u):
                act.wait_ge(t_.nmx, u + 1)
                for i in range(4):
                    nc.scalar.activation(SP[:, i, :], SP[:, i, :], ACT.Exp, bias=NMX[:, i:i + 1], accum_out=SUM[:, i:i + 1])
                nc.scalar.activation(ESK[:, :], ESK[:, :], ACT.Exp).then_inc(t_.ex, 1)

            def att_pt(u):
                act.wait_ge(t_.tr, u + 1)
                wait_done(act, t_.o, u)
                nc.scalar.activation(PT[:, 0], BANK[4][:, :].rearrange("p (i q) -> p i q", i=4), ACT.Copy).then_inc(t_.ptA, 1)

            def one_head(h):
                for t in range(4):
                    for n in range(3):
                        w = NTILE[n][1]
                        i = 3 * t + n
                        act.wait_ge(z.mm, h * 12 + (C1 + i + 1))
                        act.wait_ge(zst[i % 4], h * 48 + 16 * (3 + i // 4))
                        nc.scalar.activation(ZST[:, i % 4, 0:w], BANK[i % 2][:, 0:w], ACT.Sigmoid if t == 3 else ACT.Copy,
                                             scale=float(LD) ** -0.5 if t == 1 else 1.0).then_inc(z.ev, 1)
                        if n == 0:
                            att_exps(h * 4 + t)
                        if n == 1:
                            att_pt(h * 4 + t)
                    act.wait_ge(z.mm, h * 12 + (C1 + 3 * t + 3))
                    act.wait_ge(zin[t], h * 16 + 16 * loads_until(12 + t))
                    nc.scalar.activation(WGH[:, t], RAW4[:, t], ACT.Copy).then_inc(z.hi, 1)

            one_head(0)
            with act.Fori(1, LH) as h:
                one_head(h)
            act.wait_ge(vk.ctr, 1)
            nc.scalar.activation(CKT[:, :], BANK[7][:, 0:P], ACT.Copy).then_inc(vk.cev, 1)
            for u in (2 * NB, 2 * NB + 1):
                att_exps(u)
                att_pt(u)
            act.wait_ge(t_.ev, 2 * NB + 2)
            act.wait_ge(z.mm, C1 + 48)
            nc.scalar.activation(HH[:, 0:4, :], ATT[:, :, :], ACT.Copy).then_inc(att_hi, 1)

            def m_first(b, par, L):
                act.wait_ge(m_.d, b + 1)
                for hh in range(LH):
                    last = nc.scalar.activation(EX[0:L, hh, 0:L], EX[0:L, hh, 0:L], ACT.Exp, bias=COLS[0:L, bass.ds(b * 8 + hh, 1)])
                last.then_inc(m_.ex, 1)
                act.wait_ge(m_.kvt, b + 1)
                wait_done(act, m_.upd, b)
                for hh in range(LH):
                    last = nc.scalar.activation(KWS[0:L, hh, :], BANK[3][0:L, hh * P:(hh + 1) * P], ACT.Copy,
                                                scale=COLS[0:L, bass.ds(b * 8 + (4 + hh), 1)])
                last.then_inc(m_.kw, 1)

            def view(bank, L):
                return bank[:, 0:LH * L].rearrange("p (h c) -> p h c", h=LH)

            def m_second(b, L):
                act.wait_ge(m_.den, b + 1)
                wait_done(act, m_.v2, b)
                nc.scalar.activation(DM[:, :, 0:L], view(BANK[6], L), ACT.Abs).then_inc(m_.ad, 1)
                act.wait_ge(m_.w, b + 1)
                nc.scalar.activation(SQM[:, :, 0:L], WN[:, :, 0:L], ACT.Square).then_inc(m_.sq, 1)
                act.wait_ge(m_.dm, b + 1)
                nc.scalar.activation(DM[:, :, 0:L], DM[:, :, 0:L], ACT.Square, scale=EPS ** 0.5).then_inc(m_.d2, 1)

            def m_third(b, L, col):
                act.wait_ge(m_.v2, b + 1)
                nc.scalar.activation(RM[:, :, 0:L], RM[:, :, 0:L], ACT.Sqrt).then_inc(m_.rs, 1)
                act.wait_ge(m_.y, b + 1)
                nc.scalar.activation(HH[:, 4:8, bass.ds(col, L)], WN[:, :, 0:L], ACT.Copy).then_inc(m_.hi, 1)

            m_first(0, 0, P)

            def m_block(b, par, col):
                m_second(b, P)
                m_first(b + 1, 1 - par, P)
                m_third(b, P, col)

            m_block(0, 0, 0)
            with act.Fori(0, NB // 2 - 1) as i:
                m_block(i * 2 + 1, 1, i * (2 * P) + P)
                m_block(i * 2 + 2, 0, i * (2 * P) + 2 * P)
            for b in (NB - 1, NB):
                L = P if b < NB else DEC
                m_second(b, L)
                if b < NB:
                    m_first(b + 1, (b + 1) % 2, P if b + 1 < NB else DEC)
                m_third(b, L, b * P)

            for t in range(4):
                j = UNITS + 5 + t
                unit_high(act, t, loads_until(j), freed=C1 + 48 + 3 * t + 3)
            act.wait_ge(o_add, 3 * OUT_UNITS)
            norm_act_root(act, norm[2], 0, BANK[4])
            for c in range(4):
                ffn_act_gu_high(act, ffn[1], 0, c, first=True)
            norm_act_high(act, norm[2], 0)
            ffn_act(act, ffn[1], norm[2])

            for b in range(NB + 1):
                L = P if b < NB else DEC
                for half in range(2):
                    act.wait_ge(fin.tr, 2 * b + half + 1)
                    nc.scalar.activation(JUNK[0:L, (2 * b + half) % 4, :], BANK[(2 * b + half) % 8][0:L, :], ACT.Square, accum_out=FS[0:L, b % 4, half:half + 1]).then_inc(fin.sq, 1)
                act.wait_ge(fin.sum, b + 1)
                nc.scalar.activation(FS[0:L, b % 4, 2:3], FS[0:L, b % 4, 2:3], ACT.Sqrt, bias=EPSC[0:L, 0:1], scale=1.0 / D).then_inc(fin.rs, 1)

        @block.vector
        def _(dve):
            for b in range(NB + 1):
                L = P if b < NB else DEC
                dve.wait_ge(x_tr, 2 * b + 2)
                nc.vector.tensor_copy(X[:, 4:8, b * P:b * P + L], BANK[(2 * b + 1) % 8][:, :].rearrange("p (k c) -> p k c", k=4)[:, :, 0:L]).then_inc(x_evV, 1)
            dve.wait_ge(const_in, 16 * 12)
            nc.vector.tensor_scalar(GQ[:, 0:1], GQ[:, 0:1], float(HD) ** -0.5, None, ALU.mult)
            nc.vector.tensor_scalar(NSINK[:, :], SINK[:, :], -1.0, None, ALU.mult)
            for c in range(4):
                ffn_dve_gu_low(dve, ffn[0], 0, c)
            norm_dve(dve, norm[0], 0, 0)
            ffn_dve(dve, ffn[0], norm[0], 0)

            ffn_dve_x(dve, ffn[0], LAST, 0)
            ffn_dve_x(dve, ffn[0], LAST, 1)
            norm_dve(dve, norm[1], 0, 1)
            ffn_dve_x(dve, ffn[0], LAST, 2)
            for j in (1, 2, 3, 4):
                unit_low(dve, j, j % 4)

            normed = stored = 0
            for c, (j, n) in enumerate(M1):
                t0, w = NTILE[n]
                if c in (0, 4):
                    norm_dve(dve, norm[1], 1 + c // 4, 1)
                if j >= 3:
                    if j == 3:
                        dst, gain = KTT[:, t0:t0 + w], GQ[:, 1:2]
                    else:
                        dst, gain = ZST[:, stored % 4, 0:w], GQ[:, 0:1]
                        if stored >= 4:
                            dve.wait_ge(zst[stored % 4], 16 * (stored // 4))
                        stored += 1
                    dve.wait_ge(z.sqc, normed + 1)
                    nc.vector.tensor_scalar(dst, BANK[c % 4][:, 0:w], gain, None, ALU.mult).then_inc(z.zg, 1)
                    normed += 1
                    dve.wait_ge(z.rsc, normed)
                    nc.vector.reciprocal(RSC[:, 0:w], RSC[:, 0:w]).then_inc(z.rc, 1)
                    dve.wait_ge(z.rc, normed)
                    nc.vector.tensor_tensor(dst, dst, RSC[:, 0:w], ALU.mult).then_inc(z.scaled, 1)
                if n == 2:
                    unit_low(dve, j + 4, j % 4)
                if c == 12:
                    nc.vector.memset(R4[:, :], 1.0).then_inc(g.f, 1)
                    dve.wait_ge(g.f, 1)
                    nc.vector.memset(R4[:, 0:T:P], 0.0).then_inc(g.f, 1)
                if c == 14:
                    dve.wait_ge(g.ln, 1)
                    nc.vector.scalar_tensor_tensor(out=R2[:, :], in0=R2[:, :], scalar=0.0, in1=R3[:, :], op0=ALU.min, op1=ALU.subtract).then_inc(g.lf, 1)
                    dve.wait_ge(g.lf, 1)
                    dve.wait_ge(g.f, 2)
                    nc.vector.tensor_tensor_scan(R3[:, :], R4[:, :], R2[:, :], 0.0, ALU.mult, ALU.add).then_inc(g.b, 1)
                    dve.wait_ge(g.b, 1)
                    nc.vector.tensor_tensor_scan(R4[:, 0:SEQ], R2[:, 0:SEQ], R1[:, 0:SEQ], 0.0, ALU.add, ALU.max).then_inc(g.m, 1)
                    nc.vector.tensor_tensor_scan(R4[:, SEQ:T], R2[:, SEQ:T], R1[:, SEQ:T], GATE[:, 2:3], ALU.add, ALU.max).then_inc(g.m, 1)
                    dve.wait_ge(g.m, 2)
                    nc.vector.tensor_tensor(R1[:, :], R1[:, :], R3[:, :], ALU.subtract).then_inc(g.r, 1)
                    dve.wait_ge(g.r, 1)
                    nc.vector.tensor_tensor(R3[:, :], R3[:, :], R4[:, :], ALU.subtract).then_inc(g.u, 1)

            def att_softmax(u, g_, table):
                dve.wait_ge(t_.s, u + 1)
                wait_done(dve, t_.tr, u)
                for i, hl in enumerate(HEAD_ORDER):
                    slope = 2.0 ** -(4 * g_ + hl + 1)
                    last = nc.vector.scalar_tensor_tensor(out=SP[:, i, :], in0=table[:, :], scalar=-slope, in1=BANK[2 + i // 2][:, (i % 2) * 256:(i % 2) * 256 + 256],
                                                          op0=ALU.mult, op1=ALU.add)
                last.then_inc(t_.bias, 1)
                dve.wait_ge(t_.bias, u + 1)
                nc.vector.tensor_reduce(NMX[:, :], SP[:, :, :], AX.X, ALU.max, negate=True).then_inc(t_.nmax, 1)
                dve.wait_ge(t_.nmax, u + 1)
                order = lambda ap: ap[:, 4 * g_:4 * g_ + 4].rearrange("p (a b) -> p b a", b=2)
                nm = NMX[:, :].rearrange("p (b a) -> p b a", b=2)
                nc.vector.tensor_tensor(nm, nm, order(NSINK), ALU.min).then_inc(t_.nmin, 1)
                dve.wait_ge(t_.nmin, u + 1)
                nc.vector.tensor_tensor(ESK[:, :].rearrange("p (b a) -> p b a", b=2), nm, order(SINK), ALU.add).then_inc(t_.nmx, 1)

            def att_normalise(u):
                dve.wait_ge(t_.ex, u + 1)
                nc.vector.tensor_tensor(DEN[:, :], SUM[:, :], ESK[:, :], ALU.add).then_inc(t_.den, 1)
                dve.wait_ge(t_.den, u + 1)
                nc.vector.reciprocal(DEN[:, :], DEN[:, :]).then_inc(t_.rden, 1)
                dve.wait_ge(t_.rden, u + 1)
                for i in range(4):
                    last = nc.vector.tensor_scalar(SP[:, i, :], SP[:, i, :], DEN[:, i:i + 1], None, ALU.mult)
                last.then_inc(t_.p, 1)

            def att_out(u, g_, col, L=P):
                dve.wait_ge(t_.tr, u + 1)
                wait_done(dve, t_.o, u)
                nc.vector.tensor_copy(PT[:, 1], BANK[5][:, :].rearrange("p (i q) -> p i q", i=4)).then_inc(t_.ptV, 1)
                dve.wait_ge(t_.o, u + 1)
                nc.vector.tensor_copy(ATT[:, 2 * g_:2 * g_ + 2, bass.ds(col, L)], BANK[6][:, 0:256].rearrange("p (a q) -> p a q", a=2)[:, :, 0:L]).then_inc(t_.ev, 1)

            def att_block(h, first):
                for t in range(4):
                    u = h * 4 + t
                    att_softmax(u, t % 2, DT0 if first and t < 2 else DT)
                    att_normalise(u)
                    att_out(u, t % 2, h * (2 * P) + (t // 2) * P)
                    unit_low(dve, h * 4 + (12 + t), t)
            dve.wait_ge(const_ops, 15)
            att_block(0, True)
            with dve.Fori(1, LH) as h:
                att_block(h, False)
            for g_ in range(2):
                att_softmax(2 * NB + g_, g_, DT)
                att_normalise(2 * NB + g_)
                att_out(2 * NB + g_, g_, SEQ, DEC)
            dve.wait_ge(att_hi, 1)
            dve.wait_ge(t_.ev, 2 * NB + 2)
            nc.vector.tensor_tensor(HL[:, 0:4, :], ATT[:, :, :], HH[:, 0:4, :].bitcast(F32), ALU.subtract).then_inc(att_lo, 1)

            def view(bank, L, p=P):
                return bank[0:p, 0:LH * L].rearrange("p (h c) -> p h c", h=LH)

            def m_first(b, L):
                dve.wait_ge(m_.kvt, b + 1)
                wait_done(dve, m_.upd, b)
                nc.vector.tensor_copy(VM[0:L], view(BANK[4], P, L)).then_inc(m_.v, 1)
                dve.wait_ge(m_.ex, b + 1)
                dve.wait_ge(m_.s, b + 1)
                nc.vector.tensor_tensor(ASM[0:L, :, 0:L], EX[0:L, :, 0:L], view(BANK[2], L, L), ALU.mult).then_inc(m_.asm, 1)

            def m_second(b, par, L):
                dve.wait_ge(m_.num, b + 1)
                wait_done(dve, m_.lo, b)
                nc.vector.tensor_tensor(WN[:, :, 0:L], ZB[:, par, 12:16, 0:L], view(BANK[5], L), ALU.mult).then_inc(m_.w, 1)
                dve.wait_ge(m_.ad, b + 1)
                nc.vector.scalar_tensor_tensor(out=DM[:, :, 0:L], in0=DM[:, :, 0:L], scalar=BOUND, in1=GB[:, par, 8:12, 0:L], op0=ALU.min, op1=ALU.max).then_inc(m_.dm, 1)
                dve.wait_ge(m_.upd, b + 1)
                for hh in range(LH):
                    bank = BANK[7 if hh < 2 else 0]
                    last = nc.vector.scalar_tensor_tensor(out=CN[:, hh, :], in0=CN[:, hh, :], scalar=GB[:, par, 4 + hh, L - 1:L],
                                                          in1=bank[:, (hh % 2) * 256:(hh % 2) * 256 + 256], op0=ALU.mult, op1=ALU.add)
                last.then_inc(m_.cn, 1)

            def m_third(b, L):
                dve.wait_ge(m_.ss, b + 1)
                dve.wait_ge(m_.d2, b + 1)
                nc.vector.scalar_tensor_tensor(out=RM[:, :, 0:L], in0=view(BANK[1], L), scalar=1.0 / LD, in1=DM[:, :, 0:L], op0=ALU.mult, op1=ALU.add).then_inc(m_.v2, 1)
                dve.wait_ge(m_.rs, b + 1)
                nc.vector.reciprocal(RM[:, :, 0:L], RM[:, :, 0:L]).then_inc(m_.rc, 1)
                dve.wait_ge(m_.rc, b + 1)
                for hh in range(LH):
                    last = nc.vector.scalar_tensor_tensor(out=WN[:, hh, 0:L], in0=WN[:, hh, 0:L], scalar=GO[:, hh:hh + 1], in1=RM[:, hh, 0:L], op0=ALU.mult, op1=ALU.mult)
                last.then_inc(m_.y, 1)

            m_first(0, P)
            dve.wait_ge(m_.cz, 1)

            def m_block(b, par):
                m_second(b, par, P)
                m_first(b + 1, P)
                m_third(b, P)

            m_block(0, 0)
            with dve.Fori(0, NB // 2 - 1) as i:
                m_block(i * 2 + 1, 1)
                m_block(i * 2 + 2, 0)
            for b in (NB - 1, NB):
                L = P if b < NB else DEC
                if b == NB:
                    dve.wait_ge(m_.c0, 32)
                    nc.vector.tensor_copy(CN[:, :, P:2 * P], N0C[:, :, None].broadcast_to([P, LH, P])).then_inc(m_.n0, 1)
                    dve.wait_ge(m_.n0, 1)
                m_second(b, b % 2, L)
                if b < NB:
                    m_first(b + 1, P if b + 1 < NB else DEC)
                m_third(b, L)

            for i in range(2):
                for t in range(4):
                    for n in range(3):
                        q = 12 * i + 3 * t + n
                        dve.wait_ge(z.mm, C1 + 48 + q + 1)
                        nc.vector.tensor_tensor(x_view(4 * i + t, n), x_view(4 * i + t, n), BANK[q % 4][:, 0:NTILE[n][1]], ALU.add).then_inc(o_add, 1)
                    if i == 0:
                        unit_low(dve, UNITS + 5 + t, t)
            for c in range(4):
                ffn_dve_gu_low(dve, ffn[1], 0, c)
            norm_dve(dve, norm[2], 0, 2)
            ffn_dve(dve, ffn[1], norm[2], 2)
            for n in range(3):
                ffn_dve_x(dve, ffn[1], LAST, n)

            dve.wait_ge(fin.g, 16)
            for b in range(NB + 1):
                L = P if b < NB else DEC
                f = FS[0:L, b % 4]
                dve.wait_ge(fin.sq, 2 * b + 2)
                nc.vector.tensor_tensor(f[:, 2:3], f[:, 0:1], f[:, 1:2], ALU.add).then_inc(fin.sum, 1)
                dve.wait_ge(fin.rs, b + 1)
                nc.vector.reciprocal(f[:, 3:4], f[:, 2:3]).then_inc(fin.rc, 1)
                dve.wait_ge(fin.rc, b + 1)
                if b >= 4:
                    dve.wait_ge(fin_out[b % 4], 16 * (b // 4))
                for half in range(2):
                    c = slice(512 * half, 512 * half + 512)
                    nc.vector.scalar_tensor_tensor(out=YO[0:L, b % 4, c], in0=BANK[(2 * b + half) % 8][0:L, :], scalar=f[:, 3:4], in1=GF[0:L, c],
                                                   op0=ALU.mult, op1=ALU.mult).then_inc(fin.y, 1)

        @block.tensor
        def _(pe):
            pe.wait_ge(const_ops, 11)
            for b in range(NB + 1):
                L = P if b < NB else DEC
                if b % 4 == 0:
                    pe.wait_ge(x_in[b // 4], 16)
                for half in range(2):
                    if b >= 4:
                        pe.wait_ge(x_evV if half else x_evA, b - 3)
                    for k in range(4):
                        f0 = (4 * half + k) * P
                        tr = nc.tensor.transpose(BANK[(2 * b + half) % 8][:, k * P:k * P + L], XIN[0:L, b, f0:f0 + P], IDENT[0:L, 0:L])
                    tr.then_inc(x_tr, 1)
            pe.wait_ge(x_evA, NB + 1)
            pe.wait_ge(x_evV, NB + 1)
            norm_pe(pe, norm[0], 0, BANK[4])
            ffn_pe(pe, ffn[0], norm[0])
            ffn_pe_down(pe, ffn[0], LAST, 0)
            ffn_pe_down(pe, ffn[0], LAST, 1)
            pe.wait_ge(ffn[0].silu, 6 * PAIRS)
            norm_pe(pe, norm[1], 0, BANK[4])
            ffn_pe_down(pe, ffn[0], LAST, 2)

            pe.wait_ge(ffn[0].x_add, 24 * PAIRS)
            pe.wait_ge(ffn[0].mul, 6 * PAIRS)
            bd = []

            def head_sums(c):
                i = NORMED.index(c)
                w = NTILE[M1[c][1]][1]
                pe.wait_ge(z.sqc, i + 1)
                if i:
                    pe.wait_ge(z.rsc, i)
                nc.tensor.matmul(BANK[5][:, 0:w], BD[:, :], SQC[:, 0:w], start=True, stop=True).then_inc(z.bd, 1)

            for c, (j, n) in enumerate(M1):
                if c < 12 and c % 4 == 0:
                    pe.wait_ge(norm[1].lo, 2 * n + 2)
                pe.wait_ge(z.lo, j)
                if c >= 4:
                    if c - 4 in PLAIN:
                        pe.wait_ge(z.ev, PLAIN.index(c - 4) + 1)
                    else:
                        pe.wait_ge(z.sqc, NORMED.index(c - 4) + 1)
                        pe.wait_ge(z.zg, NORMED.index(c - 4) + 1)
                unit_chain(pe, n, j % 4, BANK[c % 4])
                if c - 1 in NORMED and c - 1 not in bd:
                    head_sums(c - 1)
                    bd.append(c - 1)
                if c in (3, 7, 11, C1 - 1):
                    head_sums(c)
                    bd.append(c)
                if c in (0, 4):
                    norm_pe(pe, norm[1], 1 + c // 4, BANK[4])
            pe.wait_ge(g.ws, NB + 1)
            for b in range(NB + 1):
                s0, s1 = b * P, min(b * P + P, T)
                for i, r in enumerate((R1, R6)):
                    tr = nc.tensor.transpose(BANK[6][0:s1 - s0, 8 * b + 4 * i:8 * b + 4 * i + 4], r[:, s0:s1], IDENT[0:LH, 0:LH])
            tr.then_inc(g.col, 1)
            pe.wait_ge(z.scaled, len(NORMED))
            for b in range(NB + 1):
                s0, s1 = b * P, min(b * P + P, T)
                bank = BANK[(7, 4, 5)[b // 4]]
                tr = nc.tensor.transpose(bank[0:s1 - s0, (b % 4) * P:(b % 4) * P + P], VT[:, s0:s1], IDENT[:, :])
                if b % 4 == 3:
                    tr.then_inc(vk.tr, 1)
            nc.tensor.transpose(BANK[5][:, P:2 * P], KTT[:, SEQ - P:SEQ], IDENT[:, :])
            nc.tensor.transpose(BANK[5][0:DEC, 2 * P:3 * P], KTT[:, SEQ:T], IDENT[:, :]).then_inc(vk.tr, 1)
            pe.wait_ge(z.zg, len(NORMED))
            pe.wait_ge(z.sqc, len(NORMED))
            pe.wait_ge(z.ev, E1)
            pe.wait_ge(vk.ev, 3)
            pe.wait_ge(g.colev, 2)

            def att_scores(u, par, g_, loads):
                pe.wait_ge(at_in[par], loads)
                wait_done(pe, t_.bias, u)
                for i, hl in enumerate(HEAD_ORDER):
                    po = hl % 2
                    rows = slice(po * HD, po * HD + HD)
                    mm = nc.tensor.matmul(BANK[2 + i // 2][:, (i % 2) * 256:(i % 2) * 256 + 256], QB[rows, par, 2 * g_ + hl // 2, :],
                                          KW[rows, par, 0 if g_ == po else 1, :], start=True, stop=True)
                mm.then_inc(t_.s, 1)

            def att_transposes(u):
                pe.wait_ge(t_.p, u + 1)
                wait_done(pe, t_.ptA, u)
                wait_done(pe, t_.ptV, u)
                for w in range(2):
                    for i in range(4):
                        tr = nc.tensor.transpose(BANK[4 + w][:, i * P:(i + 1) * P], SP[:, i, w * P:(w + 1) * P], IDENT[:, :])
                tr.then_inc(t_.tr, 1)

            def att_values(u, par, g_):
                pe.wait_ge(t_.ptA, u + 1)
                pe.wait_ge(t_.ptV, u + 1)
                wait_done(pe, t_.ev, u)
                for po in range(2):
                    for w in range(2):
                        mm = nc.tensor.matmul(BANK[6][po * HD:po * HD + HD, 0:256], VW[:, par, w, g_ * HD:g_ * HD + HD],
                                              PT[:, w, 2 * po:2 * po + 2, :], start=(w == 0), stop=(w == 1))
                mm.then_inc(t_.o, 1)

            def one_head(h):
                for t in range(4):
                    u, par, g_ = h * 4 + t, t // 2, t % 2
                    att_scores(u, par, g_, h * 80 + (80 if par else 144))
                    pe.wait_ge(z.lo, h * 4 + (8 + t))
                    for n in range(3):
                        i = 3 * t + n
                        pe.wait_ge(z.ev, h * 12 + (E1 + i - 1))
                        unit_chain(pe, n, t, BANK[i % 2])
                        if n == 1:
                            att_transposes(u)
                    att_values(u, par, g_)

            one_head(0)
            with pe.Fori(1, LH) as h:
                one_head(h)
            pe.wait_ge(vk.cin, 16)
            nc.tensor.transpose(BANK[7][:, 0:P], CKV[:, :], IDENT[:, :]).then_inc(vk.ctr, 1)
            for g_ in range(2):
                att_scores(2 * NB + g_, 0, g_, 144 + 3 * 80 + 144)
                att_transposes(2 * NB + g_)
                att_values(2 * NB + g_, 0, g_)

            def m_first(b, par, L, loads):
                pe.wait_ge(m_in[par], loads)
                wait_done(pe, m_.kw, b)
                wait_done(pe, m_.v, b)
                for bank, first in ((3, 4), (4, 8)):
                    for hh in range(LH):
                        tr = nc.tensor.transpose(BANK[bank][0:L, hh * P:(hh + 1) * P], ZB[:, par, first + hh, 0:L], IDENT[:, :])
                tr.then_inc(m_.kvt, 1)
                wait_done(pe, m_.asm, b)
                for hh in range(LH):
                    mm = nc.tensor.matmul(BANK[2][0:L, hh * L:(hh + 1) * L], ZB[:, par, 4 + hh, 0:L], ZB[:, par, hh, 0:L], start=True, stop=True)
                mm.then_inc(m_.s, 1)

            def m_second(b, L):
                pe.wait_ge(m_.v, b + 1)
                pe.wait_ge(m_.asm, b + 1)
                pe.wait_ge(m_.qw, b + 1)
                wait_done(pe, m_.cn, b)
                wait_done(pe, m_.w, b)
                for hh in range(LH):
                    out = BANK[5][:, hh * L:(hh + 1) * L]
                    nc.tensor.matmul(out, VM[0:L, hh, :], ASM[0:L, hh, 0:L], start=True, stop=False)
                    mm = nc.tensor.matmul(out, CN[:, hh, 0:P], QWI[:, hh, 0:L], start=False, stop=True)
                mm.then_inc(m_.num, 1)
                wait_done(pe, m_.ad, b)
                for hh in range(LH):
                    out = BANK[6][:, hh * L:(hh + 1) * L]
                    nc.tensor.matmul(out, ONES[0:L, :], ASM[0:L, hh, 0:L], start=True, stop=False)
                    mm = nc.tensor.matmul(out, CN[:, hh, P:2 * P], QWI[:, hh, 0:L], start=False, stop=True)
                mm.then_inc(m_.den, 1)
                pe.wait_ge(m_.kw, b + 1)
                for hh in range(LH):
                    bank, c = BANK[7 if hh < 2 else 0], (hh % 2) * 256
                    nc.tensor.matmul(bank[:, c:c + P], KWS[0:L, hh, :], VM[0:L, hh, :], start=True, stop=True)
                    mm = nc.tensor.matmul(bank[:, c + P:c + 2 * P], KWS[0:L, hh, :], ONES[0:L, :], start=True, stop=True)
                mm.then_inc(m_.upd, 1)

            def m_third(b, L):
                pe.wait_ge(m_.sq, b + 1)
                wait_done(pe, m_.v2, b)
                nc.tensor.matmul(BANK[1][:, 0:LH * L], ONES[:, :], SQM[:, :, 0:L], start=True, stop=True).then_inc(m_.ss, 1)

            pe.wait_ge(z.ev, E1 + 48)
            pe.wait_ge(t_.ev, 2 * NB + 2)
            m_first(0, 0, P, 32)
            pe.wait_ge(m_.cz, 1)

            def m_block(b, par, next_loads):
                m_second(b, P)
                m_first(b + 1, 1 - par, P, next_loads)
                m_third(b, P)

            m_block(0, 0, 32)
            with pe.Fori(0, NB // 2 - 1) as i:
                m_block(i * 2 + 1, 1, i * 32 + 64)
                m_block(i * 2 + 2, 0, i * 32 + 64)
            for b in (NB - 1, NB):
                L = P if b < NB else DEC
                if b == NB:
                    pe.wait_ge(m_.n0, 1)
                m_second(b, L)
                if b < NB:
                    m_first(b + 1, (b + 1) % 2, P if b + 1 < NB else DEC, 32 * ((b + 1) // 2 + 1))
                m_third(b, L)

            pe.wait_ge(m_.lo, NB + 1)
            pe.wait_ge(m_.v2, NB + 1)
            for q in range(3 * OUT_UNITS):
                j, n = q // 3, q % 3
                if n == 0:
                    pe.wait_ge(z.lo, UNITS + 1 + j)
                if q >= 4:
                    pe.wait_ge(o_add, q - 3)
                unit_chain(pe, n, j % 4, BANK[q % 4])
            norm_pe(pe, norm[2], 0, BANK[4])
            pe.wait_ge(o_add, 3 * OUT_UNITS)
            ffn_pe(pe, ffn[1], norm[2])
            for n in range(3):
                ffn_pe_down(pe, ffn[1], LAST, n)

            pe.wait_ge(ffn[1].x_add, 24 * PAIRS)
            for b in range(NB + 1):
                L = P if b < NB else DEC
                if b >= 4:
                    pe.wait_ge(fin.y, 2 * (b - 3))
                for half in range(2):
                    for k in range(4):
                        tr = nc.tensor.transpose(BANK[(2 * b + half) % 8][0:L, k * P:(k + 1) * P], X[:, 4 * half + k, b * P:b * P + L], IDENT[:, :])
                    tr.then_inc(fin.tr, 1)


_INS = ["x_prompt", "x_sample", "cache_k", "cache_v", "state_C", "state_n", "state_m", "g_ffn1", "w1_gate", "w1_up", "w1_down",
        "g_mix", "w_in", "b_igate", "b_fgate", "g_q", "g_k", "attn_sinks", "g_lstm_out", "w_out", "g_ffn2", "w2_gate", "w2_up",
        "w2_down", "g_final"]
_ROWS = (1, 1, P, KV, HD)
_OUTS = [(1, SEQ, D), (1, DEC, D),
         _ROWS, _ROWS, (1, 1, LH, LD, LD), (1, 1, LH, LD), (1, 1, LH),
         _ROWS, _ROWS, (1, 1, LH, LD, LD), (1, 1, LH, LD), (1, 1, LH)]


def kernel(**inputs):
    import numpy as _np
    import concourse.bacc as _bacc
    from concourse import mybir as _mybir
    from concourse.bass_utils import run_bass_kernel_spmd as _run

    nc = _bacc.Bacc("TRN2", target_bir_lowering=False, num_devices=1)
    arrays, ins = {}, {}
    for name in _INS:
        x = _np.ascontiguousarray(inputs[name])
        arrays[f"in_{name}"] = x
        ins[name] = nc.dram_tensor(f"in_{name}", x.shape, _mybir.dt.from_np(x.dtype), kind="ExternalInput").ap()
    outs = [nc.dram_tensor(f"out_{i}", shape, _mybir.dt.float32, kind="ExternalOutput").ap() for i, shape in enumerate(_OUTS)]
    build(nc, ins, outs)
    r = _run(nc, [arrays], core_ids=[0])
    return tuple(r.results[0][f"out_{i}"] for i in range(len(_OUTS)))
```

```python
import concourse.bass as bass
from concourse import mybir
from collections import namedtuple
from contextlib import ExitStack

F32 = mybir.dt.float32
F32R = mybir.dt.float32r
ACT = mybir.ActivationFunctionType
ALU = mybir.AluOpType
AX = mybir.AxisListType

P = 128
D = 1024
KT = D // P
SEQ, DEC = 1024, 64
T = SEQ + DEC
NB = SEQ // P
NTILE = [(0, 364), (364, 362), (726, 362)]
NW = 364
FF = 2816
PAIRS = FF // (2 * P)
HEADS, KV, HD = 8, 2, 64
LH, LD = 4, 128
EPS = 1e-6
MASKED = 1e30
BOUND = 1e18
Q0, K0, V0, M0 = 0, 512, 640, 768
G0 = M0 + 4 * LH * LD
UNITS = 23
OUT_UNITS = KT


def wait_done(engine, semaphore, count):
    if not isinstance(count, int) or count > 0:
        engine.wait_ge(semaphore, count)


def build(nc, a, o):
    with ExitStack() as ctx:
        ctx.enter_context(nc.allow_non_contiguous_dma(reason="gains, biases and states: a few small transfers"))
        base = (nc.sbuf_base + 63) // 64 * 64
        at = {}

        def place(name, shape, dtype, offset):
            return nc.alloc_sbuf_tensor_at(name, shape, dtype, offset=base + offset)

        def region(name, size):
            at[name] = at.get("end", 0)
            at["end"] = at[name] + size
            return at[name]

        def sem(name):
            return ctx.enter_context(nc.semaphore(name))

        rX = region("x", KT * T * 4)
        rHH = region("hh", KT * T * 4)
        rHL = region("hl", KT * T * 4)
        rA = region("a", 4 * T * 4)
        rWG = region("wg", 2 * 4 * 4096)
        rRAW = region("raw", 4 * 4096)
        rD = region("d", 3 * 8192)
        rT = region("t", 8 * NW * 4)
        rC = region("c", 0)
        assert base + rC < nc.sbuf_usable_end

        X = place("X", [P, KT, T], F32, rX)
        HH = place("HH", [P, KT, T], F32R, rHH)
        HL = place("HL", [P, KT, T], F32R, rHL)
        XIN = place("XIN", [P, NB + 1, D], F32, rHH)
        AH = place("AH", [P, 2, T], F32R, rA)
        AL = place("AL", [P, 2, T], F32R, rA + 2 * T * 4)
        ATT = place("ATT", [P, 4, T], F32, rA)
        WGH = place("WGH", [P, 4, KT, P], F32R, rWG)
        WGL = place("WGL", [P, 4, KT, P], F32R, rWG + 4 * 4096)
        RAWG = place("RAWG", [P, KT, 2 * P], F32, rRAW)
        RAWU = place("RAWU", [P, KT, 2 * P], F32, rRAW + 8192)
        RAW4 = place("RAW4", [P, 4, KT, P], F32, rRAW)
        WDH = place("WDH", [P, 2, D], F32R, rD)
        WDL = place("WDL", [P, 2, D], F32R, rD + 8192)
        RAWD = place("RAWD", [P, 2, D], F32, rD + 16384)
        SQ = [place("SQa", [P, 4, NW], F32, rD + 16384), place("SQb", [P, 4, NW], F32, rT + 4 * NW * 4)]
        RS = place("RS", [P, NW], F32, rD + 16384 + 4 * NW * 4)
        ST = place("ST", [P, 2, NW], F32, rT)
        AT = place("AT", [P, 2, NW], F32, rT + 2 * NW * 4)

        ZST = place("ZST", [P, 4, NW], F32, rT)
        R1, R2, R3, R4 = (place(f"R{i + 1}", [LH, T], F32, rA + i * T * 4) for i in range(4))
        R5, R6 = (place(f"R{i + 5}", [LH, T], F32, rD + 3 * 8192 - (2 - i) * T * 4) for i in range(2))
        VT = place("VT", [P, T], F32, rD)
        KTT = place("KTT", [P, T], F32, rD + T * 4)
        SQC = place("SQC", [P, NW], F32, rD + 2 * T * 4)
        RSC = place("RSC", [P, NW], F32, rD + 2 * T * 4 + 1472)
        assert 4 * T * 4 + 2 * 1472 <= 3 * 8192 and 2 * T * 4 + 2 * 1472 <= 2 * 8192
        VTOK = place("VTOK", [P, NB + 1, P], F32, rA)
        KTOK = place("KTOK", [P, 2, P], F32, rA + (NB + 1) * 512)

        QB = place("QB", [P, 2, 4, P], F32, rD)
        KW = place("KW", [P, 2, 2, 2 * P], F32, rD + 4096)
        VW = place("VW", [P, 2, 2, P], F32, rD + 8192)
        SP = place("SP", [P, 4, 2 * P], F32, rD + 10240)
        PT = place("PT", [P, 2, 4, P], F32, rD + 14336)
        CKV = place("CKV", [P, P], F32, rD + 18432)
        CKT = place("CKT", [P, P], F32, rD + 18944)
        ZQ = place("ZQ", [P, 2, 12, P], F32, rD)
        ZO = place("ZO", [P, 2, LH, P], F32, rD + 12288)
        EX = place("EX", [P, 2, LH, P], F32, rD + 16384)
        GU = place("GU", [P, 2, 8, P], F32, rA)
        GM = place("GM", [P, 2, LH, P], F32, rA + 8192)
        CN = place("CN", [P, LH, 2 * P], F32, rA + 12288)
        N0C = place("N0C", [P, LH], F32, rA + 16384)
        DECAY = place("DECAY", [P, 2, LH], F32, rA + 16416)
        ASM = place("ASM", [P, 2, LH, P], F32, rWG)
        QWI = place("QWI", [P, 2, LH, P], F32, rWG + 4096)
        KWS = place("KWS", [P, 2, LH, P], F32, rWG + 8192)
        VM = place("VM", [P, 2, LH, P], F32, rWG + 12288)
        WN = place("WN", [P, LH, P], F32, rT)
        SQM = place("SQM", [P, LH, P], F32, rT + 2048)
        DM = place("DM", [P, LH, P], F32, rT + 4096)
        RM = place("RM", [P, LH, P], F32, rT + 6144)
        YO = place("YO", [P, 4, D], F32, rHH)
        GF = place("GF", [P, D], F32, rD)
        JUNK = place("JUNK", [P, 4, 512], F32, rT)

        IDENT = place("IDENT", [P, P], F32, rC)
        ONES = place("ONES", [P, P], F32, rC + 512)
        BD = place("BD", [P, P], F32, rC + 1024)
        DT = place("DT", [P, 2 * P], F32, rC + 1536)
        DTI = place("DTI", [P, 2 * P], mybir.dt.int32, rD)
        DT0 = place("DT0", [P, 2 * P], F32, rC + 2560)
        MC = place("MC", [P, P], F32, rC + 3584)
        COLS = place("COLS", [P, (NB + 1) * 8], F32, rC + 4096)
        small_at = rC + 4096 + (NB + 1) * 32

        def small(name, shape, partitions=P):
            nonlocal small_at
            size = 4
            for x in shape:
                size *= x
            tile = place(name, [partitions, *shape], F32, small_at)
            small_at += (size + 31) // 32 * 32
            return tile

        GC = small("GC", [3, KT])
        GQ = small("GQ", [2])
        GO = small("GO", [LH])
        SINK = small("SINK", [HEADS])
        NSINK = small("NSINK", [HEADS])
        GATE = small("GATE", [4], LH)
        GBF = small("GBF", [1], 32 + LH)
        EPSC = small("EPSC", [1])
        NMX = small("NMX", [4])
        SUM = small("SUM", [4])
        ESK = small("ESK", [4])
        DEN = small("DEN", [4])
        FS = small("FS", [4, 4])
        assert base + small_at <= nc.sbuf_usable_end

        BANK = [ctx.enter_context(nc.psum_tensor(f"bank{i}", [P, 512], F32)) for i in range(8)]

        zqk = nc.dram_tensor("zqk", (5, P, T), F32, kind="Internal").ap()
        vtok = nc.dram_tensor("vtok", (NB + 1, P, P), F32, kind="Internal").ap()
        zm = nc.dram_tensor("zm", (4 * LH, P, T), F32, kind="Internal").ap()
        grow = nc.dram_tensor("grow", (3, LH, T), F32, kind="Internal").ap()

        const_in, const_ops, dist_abs = sem("const_in"), sem("const_ops"), sem("dist_abs")
        x_in = [sem(f"x_in{i}") for i in range(3)]
        x_tr, x_evA, x_evV = sem("x_tr"), sem("x_evA"), sem("x_evV")

        def named(prefix, names):
            return namedtuple(prefix, names)(*[sem(f"{prefix}_{n}") for n in names.split()])

        ffn = [named(f"f{i}", "gu_in d_in w_hi w_lo gu_mm d_mm silu mul a_hi a_ready x_add") for i in (1, 2)]
        norm = [named(f"n{i}", "sq ss rs rc ht hi lo0 lo1") for i in range(3)]
        zin = [sem(f"z_in{s}") for s in range(4)]
        z = named("z", "padded hi lo mm ev sqc bd rsc zg rc scaled")
        zst = [sem(f"zst{s}") for s in range(4)]
        g = named("g", "f ab e ln lf b m r u w ws col colev out")
        vk = named("vk", "tr ev out kout cst cin ctr cev pad")
        at_in = [sem("at_in0"), sem("at_in1")]
        t_ = named("att", "s bias nmax nmin nmx ex den rden p tr ptA ptV o ev")
        ma_in = [sem("ma_in0"), sem("ma_in1")]
        mb_in = [sem("mb_in0"), sem("mb_in1")]
        m_ = named("m", "d qw ex kvt kw v s asm num den cn w sq ss ad dm d2 v2 rs rc y hi lo c0 n0 cz cout")
        att_hi, att_lo, o_add = sem("att_hi"), sem("att_lo"), sem("o_add")
        fin = named("fin", "tr sq sum rs rc y")
        fin_out = [sem(f"fin_out{i}") for i in range(4)]

        def x_view(k, n):
            t0, w = NTILE[n]
            return X[:, k, t0:t0 + w]

        def three_pass(bank, w, w_hi, w_lo, rhs_hi, rhs_lo, first, last):
            nc.tensor.matmul(bank[:, 0:w], w_hi, rhs_hi, start=first, stop=False)
            nc.tensor.matmul(bank[:, 0:w], w_hi, rhs_lo, start=False, stop=False)
            return nc.tensor.matmul(bank[:, 0:w], w_lo, rhs_hi, start=False, stop=last)

        def norm_act_root(act, s, n, bank):
            t0, w = NTILE[n]
            for h in range(2):
                if n:
                    act.wait_ge(s.lo1 if h else s.lo0, n)
                nc.scalar.activation(SQ[h][:, :, 0:w], X[:, 4 * h:4 * h + 4, t0:t0 + w], ACT.Square).then_inc(s.sq, 1)
            act.wait_ge(s.ss, n + 1)
            nc.scalar.activation(RS[:, 0:w], bank[:, 0:w], ACT.Sqrt, bias=EPSC[:, 0:1], scale=1.0 / D).then_inc(s.rs, 1)

        def norm_act_high(act, s, n):
            t0, w = NTILE[n]
            for h in range(2):
                act.wait_ge(s.ht, 2 * n + h + 1)
                nc.scalar.activation(HH[:, 4 * h:4 * h + 4, t0:t0 + w], SQ[h][:, :, 0:w], ACT.Copy).then_inc(s.hi, 1)

        def norm_pe(pe, s, n, bank):
            w = NTILE[n][1]
            if n:
                pe.wait_ge(s.rs, n)
            for k in range(KT):
                if k % 4 == 0:
                    pe.wait_ge(s.sq, 2 * n + k // 4 + 1)
                mm = nc.tensor.matmul(bank[:, 0:w], ONES[:, :], SQ[k // 4][:, k % 4, 0:w], start=(k == 0), stop=(k == KT - 1))
            mm.then_inc(s.ss, 1)

        def norm_dve(dve, s, n, which):
            w = NTILE[n][1]
            dve.wait_ge(s.rs, n + 1)
            nc.vector.reciprocal(RS[:, 0:w], RS[:, 0:w]).then_inc(s.rc, 1)
            dve.wait_ge(s.rc, n + 1)
            for k in range(KT):
                ht = nc.vector.scalar_tensor_tensor(out=SQ[k // 4][:, k % 4, 0:w], in0=x_view(k, n), scalar=GC[:, which, k:k + 1],
                                                    in1=RS[:, 0:w], op0=ALU.mult, op1=ALU.mult)
                if k % 4 == 3:
                    ht.then_inc(s.ht, 1)

        def norm_low(engine, tensor_tensor, s, n, h):
            t0, w = NTILE[n]
            engine.wait_ge(s.hi, 2 * n + h + 1)
            tensor_tensor(HL[:, 4 * h:4 * h + 4, t0:t0 + w], SQ[h][:, :, 0:w], HH[:, 4 * h:4 * h + 4, t0:t0 + w].bitcast(F32),
                          ALU.subtract).then_inc(s.lo1 if h else s.lo0, 1)

        def norm_pool(pool, s, n):
            norm_low(pool, nc.gpsimd.tensor_tensor, s, n, 0)

        def norm_dve_low(dve, s, n):
            norm_low(dve, nc.vector.tensor_tensor, s, n, 1)

        def norm_wait(engine, s, n):
            engine.wait_ge(s.lo0, n + 1)
            engine.wait_ge(s.lo1, n + 1)

        def ffn_sp(sp, s, w_gate, w_up, w_down, before_gu, before_d):
            def gu(col):
                for raw, w in ((RAWG, w_gate), (RAWU, w_up)):
                    sp.dma_start(raw[:, :, :], w[:, bass.ds(col, 2 * P)].rearrange("(k p) c -> p k c", p=P)).then_inc(s.gu_in, 16)

            def down(row):
                sp.dma_start(RAWD[:, :, :], w_down[bass.ds(row, 2 * P), :].rearrange("(k p) c -> p k c", p=P)).then_inc(s.d_in, 16)

            before_gu()
            gu(0)
            before_d()
            down(0)
            with sp.Fori(1, PAIRS) as p:
                sp.wait_ge(s.w_lo, p * 6 - 2)
                gu(p * (2 * P))
                sp.wait_ge(s.w_lo, p * 6)
                down(p * (2 * P))

        def raw_gu(c):
            raw = RAWU if c % 2 else RAWG
            return raw[:, :, (c // 2) * P:(c // 2 + 1) * P]

        def ffn_act_gu_high(act, s, p, c, first=False):
            act.wait_ge(s.gu_in, p * 32 + 32)
            if not first:
                act.wait_ge(s.gu_mm, p * 12 - 4 + c + 1)
            nc.scalar.activation(WGH[:, c], raw_gu(c), ACT.Copy).then_inc(s.w_hi, 1)

        def ffn_dve_gu_low(dve, s, p, c):
            dve.wait_ge(s.w_hi, p * 6 + c + 1)
            nc.vector.tensor_tensor(WGL[:, c], raw_gu(c), WGH[:, c].bitcast(F32), ALU.subtract).then_inc(s.w_lo, 1)

        def ffn_act_down_high(act, s, p, d, first=False):
            act.wait_ge(s.d_in, p * 16 + 16)
            if not first:
                act.wait_ge(s.d_mm, p * 24)
            nc.scalar.activation(WDH[:, d], RAWD[:, d], ACT.Copy).then_inc(s.w_hi, 1)

        def ffn_dve_down_low(dve, s, p, d):
            dve.wait_ge(s.w_hi, p * 6 + 4 + d + 1)
            nc.vector.tensor_tensor(WDL[:, d], RAWD[:, d], WDH[:, d].bitcast(F32), ALU.subtract).then_inc(s.w_lo, 1)

        def ffn_pe_gu(pe, s, p, n, c, first=False):
            t0, w = NTILE[n]
            t = c // 2
            pe.wait_ge(s.w_lo, p * 6 + c + 1)
            if not (first and n == 0):
                pe.wait_ge(s.mul if c % 2 else s.silu, p * 6 + 2 * n + t - 1)
            for k in range(KT):
                mm = three_pass(BANK[4 + c], w, WGH[:, c, k], WGL[:, c, k], HH[:, k, t0:t0 + w], HL[:, k, t0:t0 + w], k == 0, k == KT - 1)
            mm.then_inc(s.gu_mm, 1)

        def ffn_pe_down(pe, s, p, n):
            t0, w = NTILE[n]
            pe.wait_ge(s.a_ready, p * 6 + 2 * n + 2)
            if n == 0:
                pe.wait_ge(s.w_lo, p * 6 + 6)
            for m in range(KT):
                if n or m >= 4:
                    pe.wait_ge(s.x_add, p * 24 + 8 * n + m - 3)
                for d in range(2):
                    c = slice(m * P, m * P + P)
                    mm = three_pass(BANK[m % 4], w, WDH[:, d, c], WDL[:, d, c], AH[:, d, t0:t0 + w], AL[:, d, t0:t0 + w], d == 0, d == 1)
                mm.then_inc(s.d_mm, 1)

        def ffn_act_silu(act, s, p, n, t, first=False):
            w = NTILE[n][1]
            act.wait_ge(s.gu_mm, p * 12 + 4 * n + 2 * t + 1)
            if not (first and n == 0):
                act.wait_ge(s.mul, p * 6 + 2 * n + t - 1)
            nc.scalar.activation(ST[:, t, 0:w], BANK[4 + 2 * t][:, 0:w], ACT.Silu).then_inc(s.silu, 1)

        def ffn_dve_a(dve, s, p, n, t, first=False):
            t0, w = NTILE[n]
            dve.wait_ge(s.silu, p * 6 + 2 * n + t + 1)
            dve.wait_ge(s.gu_mm, p * 12 + 4 * n + 2 * t + 2)
            nc.vector.tensor_tensor(AT[:, t, 0:w], ST[:, t, 0:w], BANK[5 + 2 * t][:, 0:w], ALU.mult).then_inc(s.mul, 1)
            dve.wait_ge(s.mul, p * 6 + 2 * n + t + 1)
            if not first:
                dve.wait_ge(s.d_mm, p * 24 - 24 + 8 * n + 8)
            nc.vector.tensor_copy(AH[:, t, t0:t0 + w], AT[:, t, 0:w]).then_inc(s.a_hi, 1)
            dve.wait_ge(s.a_hi, p * 6 + 2 * n + t + 1)
            nc.vector.tensor_tensor(AL[:, t, t0:t0 + w], AT[:, t, 0:w], AH[:, t, t0:t0 + w].bitcast(F32), ALU.subtract).then_inc(s.a_ready, 1)

        def ffn_dve_x(dve, s, p, n, tiles=range(KT)):
            w = NTILE[n][1]
            for m in tiles:
                dve.wait_ge(s.d_mm, p * 24 + 8 * n + m + 1)
                nc.vector.scalar_tensor_tensor(out=x_view(m, n), in0=BANK[m % 4][:, 0:w], scalar=0.5, in1=x_view(m, n),
                                               op0=ALU.mult, op1=ALU.add).then_inc(s.x_add, 1)

        def ffn_act(act, s, ns):
            for n in range(3):
                if n < 2:
                    norm_act_root(act, ns, n + 1, BANK[0])
                if n == 2:
                    for d in range(2):
                        ffn_act_down_high(act, s, 0, d, first=True)
                for t in range(2):
                    ffn_act_silu(act, s, 0, n, t, first=True)
                    if n == 2:
                        ffn_act_gu_high(act, s, 1, 2 * t)
                        ffn_act_gu_high(act, s, 1, 2 * t + 1)
                    elif t == 0:
                        norm_act_high(act, ns, n + 1)

            def body(p, last):
                for n in range(3):
                    if n == 2:
                        for d in range(2):
                            ffn_act_down_high(act, s, p, d)
                    for t in range(2):
                        ffn_act_silu(act, s, p, n, t)
                        if n == 2 and not last:
                            ffn_act_gu_high(act, s, p + 1, 2 * t)
                            ffn_act_gu_high(act, s, p + 1, 2 * t + 1)
            with act.Fori(1, PAIRS - 1) as p:
                body(p, False)
            body(PAIRS - 1, True)

        def ffn_dve(dve, s, ns, which):
            for n in range(3):
                if n < 2:
                    norm_dve(dve, ns, n + 1, which)
                if n == 2:
                    for d in range(2):
                        ffn_dve_down_low(dve, s, 0, d)
                for t in range(2):
                    ffn_dve_a(dve, s, 0, n, t, first=True)
                    if n == 2:
                        ffn_dve_gu_low(dve, s, 1, 2 * t)
                        ffn_dve_gu_low(dve, s, 1, 2 * t + 1)
                    elif t == 0:
                        norm_dve_low(dve, ns, n + 1)

            def body(p, last):
                for n in range(3):
                    ffn_dve_x(dve, s, p - 1, n)
                    if n == 2:
                        for d in range(2):
                            ffn_dve_down_low(dve, s, p, d)
                    for t in range(2):
                        ffn_dve_a(dve, s, p, n, t)
                        if n == 2 and not last:
                            ffn_dve_gu_low(dve, s, p + 1, 2 * t)
                            ffn_dve_gu_low(dve, s, p + 1, 2 * t + 1)
            with dve.Fori(1, PAIRS - 1) as p:
                body(p, False)
            body(PAIRS - 1, True)

        def ffn_pe(pe, s, ns):
            for n in range(3):
                norm_wait(pe, ns, n)
                for c in range(4):
                    ffn_pe_gu(pe, s, 0, n, c, first=True)
                    if c == 0 and n < 2:
                        norm_pe(pe, ns, n + 1, BANK[0])
            with pe.Fori(1, PAIRS) as p:
                for n in range(3):
                    ffn_pe_down(pe, s, p - 1, n)
                    for c in range(4):
                        ffn_pe_gu(pe, s, p, n, c)

        LAST = PAIRS - 1

        def unit_high(act, slot, loads, freed=None):
            if freed is not None:
                act.wait_ge(z.mm, freed)
            act.wait_ge(zin[slot], loads * 16)
            nc.scalar.activation(WGH[:, slot], RAW4[:, slot], ACT.Copy).then_inc(z.hi, 1)

        def unit_low(dve, j, slot):
            dve.wait_ge(z.hi, j)
            nc.vector.tensor_tensor(WGL[:, slot], RAW4[:, slot], WGH[:, slot].bitcast(F32), ALU.subtract).then_inc(z.lo, 1)

        def loads_until(j):
            return (j - 4) // 4 + 1 if j % 4 == 0 else (j - j % 4) // 4 + 1 + (j % 4 == 1)

        def unit_chain(pe, n, slot, bank):
            t0, w = NTILE[n]
            for k in range(KT):
                mm = three_pass(bank, w, WGH[:, slot, k], WGL[:, slot, k], HH[:, k, t0:t0 + w], HL[:, k, t0:t0 + w], k == 0, k == KT - 1)
            mm.then_inc(z.mm, 1)

        M1 = [(j, n) for n in range(3) for j in (1, 2, 3, 4)] + [(j, n) for j in (5, 6, 7) for n in range(3)]
        PLAIN = [c for c, (j, n) in enumerate(M1) if j < 3]
        NORMED = [c for c, (j, n) in enumerate(M1) if j >= 3]
        STORED = [c for c, (j, n) in enumerate(M1) if j >= 4]
        C1 = len(M1)
        E1 = len(PLAIN)
        HEAD_ORDER = (0, 2, 1, 3)

        block = ctx.enter_context(nc.Block())

        @block.sync
        def _(sp):
            sp.dma_start(XIN[:, 0:4, :], a["x_prompt"][0, 0:512, :].rearrange("(b p) f -> p b f", p=P)).then_inc(x_in[0], 16)
            sp.dma_start(XIN[:, 4:8, :], a["x_prompt"][0, 512:1024, :].rearrange("(b p) f -> p b f", p=P)).then_inc(x_in[1], 16)
            sp.dma_start(XIN[0:DEC, 8, :], a["x_sample"][0, :, :]).then_inc(x_in[2], 16)

            ffn_sp(sp, ffn[0], a["w1_gate"][0], a["w1_up"][0], a["w1_down"][0],
                   lambda: None, lambda: norm_wait(sp, norm[0], 2))

            w_in, w_out = a["w_in"][0], a["w_out"][0]
            sp.wait_ge(ffn[0].w_lo, 6 * PAIRS - 2)
            sp.wait_ge(z.padded, 1)
            for gate in range(2):
                col = G0 + gate * LH
                sp.dma_start(RAW4[:, 1, :, 32 * gate:32 * gate + LH], w_in[:, col:col + LH].rearrange("(k p) c -> p k c", p=P)).then_inc(zin[1], 16)

            def load(slot, w, col):
                sp.dma_start(RAW4[:, slot], w[:, bass.ds(col, P)].rearrange("(k p) c -> p k c", p=P)).then_inc(zin[slot], 16)

            for j, col in ((2, V0), (3, K0), (4, Q0)):
                load(j % 4, w_in, col)
            for j in (5, 6, 7):
                sp.wait_ge(z.lo, j - 4)
                load(j % 4, w_in, Q0 + (j - 4) * P)
            with sp.Fori(0, LH) as h:
                for t in range(4):
                    sp.wait_ge(z.lo, h * 4 + (t + 4))
                    load(t, w_in, h * P + (M0 + t * LH * P))
            for t in range(4):
                sp.wait_ge(z.lo, UNITS - 3 + t)
                load(t, w_out, t * P)

            rows = grow.rearrange("i h c -> (i h) c")

            def m_load_first(par, col, width=P):
                sp.dma_start(ZQ[:, par, :, 0:width], zm[0:12, :, bass.ds(col, width)].rearrange("t p c -> p t c")).then_inc(ma_in[par], 16)
                sp.dma_start(GU[:, par, :, 0:width], rows[0:8, bass.ds(col, width)].partition_broadcast(P)).then_inc(ma_in[par], 16)

            def m_load_second(par, col, width=P):
                sp.dma_start(ZO[:, par, :, 0:width], zm[12:16, :, bass.ds(col, width)].rearrange("t p c -> p t c")).then_inc(mb_in[par], 16)
                sp.dma_start(GM[:, par, :, 0:width], rows[8:12, bass.ds(col, width)].partition_broadcast(P)).then_inc(mb_in[par], 16)

            def m_reload(b, par, col, width=P):
                sp.wait_ge(m_.kw, b + 1)
                sp.wait_ge(m_.asm, b + 1)
                sp.wait_ge(m_.qw, b + 1)
                m_load_first(par, col, width)
                sp.wait_ge(m_.dm, b + 1)
                m_load_second(par, col, width)

            for q in range(4):
                sp.wait_ge(zst[q], 16 * (3 + 12))
            sp.wait_ge(t_.ev, 2 * NB + 2)
            sp.wait_ge(att_lo, 1)
            sp.wait_ge(g.out, 16 * 5)
            for par in range(2):
                m_load_first(par, par * P)
                m_load_second(par, par * P)
            with sp.Fori(0, NB // 2 - 1) as i:
                for par in range(2):
                    m_reload(i * 2 + par, par, i * (2 * P) + (2 + par) * P)
            m_reload(NB - 2, 0, SEQ, DEC)

            for t in range(4):
                sp.wait_ge(z.lo, UNITS + 1 + t)
                load(t, w_out, (4 + t) * P)

            ffn_sp(sp, ffn[1], a["w2_gate"][0], a["w2_up"][0], a["w2_down"][0],
                   lambda: sp.wait_ge(z.lo, UNITS + OUT_UNITS), lambda: norm_wait(sp, norm[2], 2))

            for b in range(NB + 1):
                sp.wait_ge(fin.y, 2 * b + 2)
                if b < NB:
                    sp.dma_start(o[0][0, b * P:(b + 1) * P, :], YO[:, b % 4, :]).then_inc(fin_out[b % 4], 16)
                else:
                    sp.dma_start(o[1][0, :, :], YO[0:DEC, b % 4, :]).then_inc(fin_out[b % 4], 16)
            for i in range(4):
                sp.wait_ge(fin_out[i], 16 * ((NB - i) // 4 + 1))

        @block.gpsimd
        def _(pool):
            def const(dst, src):
                pool.dma_start(dst, src).then_inc(const_in, 16)
            for i, name in enumerate(("g_ffn1", "g_mix", "g_ffn2")):
                const(GC[:, i, :], a[name][0].rearrange("(k p) -> p k", p=P))
            for c, name in enumerate(("g_q", "g_k")):
                for half in range(2):
                    const(GQ[half * HD:(half + 1) * HD, c:c + 1], a[name].rearrange("o p -> p o"))
            const(GO[:, :], a["g_lstm_out"][0].rearrange("h p -> p h"))
            const(SINK[:, :], a["attn_sinks"][0].partition_broadcast(P))
            const(GATE[:, 0:1], a["b_igate"].rearrange("o p -> p o"))
            const(GBF[32:32 + LH, 0:1], a["b_fgate"].rearrange("o p -> p o"))
            const(GATE[:, 2:3], a["state_m"][0].rearrange("o p -> p o"))

            nc.gpsimd.memset(IDENT[:, :], 0.0).then_inc(const_ops, 1)
            nc.gpsimd.memset(ONES[:, :], 1.0).then_inc(const_ops, 1)
            nc.gpsimd.memset(BD[:, :], 0.0).then_inc(const_ops, 1)
            nc.gpsimd.memset(MC[:, :], 0.0).then_inc(const_ops, 1)
            nc.gpsimd.memset(EPSC[:, :], EPS).then_inc(const_ops, 1)
            nc.gpsimd.iota(DTI[:, :], [[-1, 2 * P]], base=P, channel_multiplier=1).then_inc(const_ops, 1)
            pool.wait_ge(const_ops, 6)
            nc.gpsimd.affine_select(out=IDENT[:, :], in_=IDENT[:, :], compare_op=ALU.not_equal, fill=1.0, base=0,
                                    pattern=[[-1, P]], channel_multiplier=1).then_inc(const_ops, 1)
            nc.gpsimd.affine_select(out=MC[:, :], in_=MC[:, :], compare_op=ALU.is_ge, fill=-MASKED, base=0,
                                    pattern=[[1, P]], channel_multiplier=-1).then_inc(const_ops, 1)
            pool.wait_ge(const_ops, 8)
            nc.gpsimd.memset(GATE[:, 1:2], 0.0).then_inc(const_ops, 1)
            pool.wait_ge(const_ops, 9)
            nc.gpsimd.memset(BD[0:HD, 0:HD], 1.0).then_inc(const_ops, 1)
            pool.wait_ge(const_ops, 10)
            nc.gpsimd.memset(BD[HD:P, HD:P], 1.0).then_inc(const_ops, 1)
            pool.wait_ge(const_ops, 11)
            pool.wait_ge(dist_abs, 1)
            nc.gpsimd.memset(DT[0:HD, 3 * HD:4 * HD], MASKED).then_inc(const_ops, 1)
            pool.wait_ge(const_ops, 12)
            nc.gpsimd.memset(DT[HD:P, 0:HD], MASKED).then_inc(const_ops, 1)
            pool.wait_ge(const_ops, 13)
            nc.gpsimd.tensor_copy(DT0[:, P:2 * P], DT[:, P:2 * P]).then_inc(const_ops, 1)
            nc.gpsimd.memset(DT0[:, 0:P], MASKED).then_inc(const_ops, 1)

            for n in range(3):
                norm_pool(pool, norm[0], n)
            pool.dma_start(o[7][0, 0, 0:HD], a["cache_k"][0, 0, HD:P]).then_inc(vk.cst, 16)
            pool.dma_start(o[8][0, 0, 0:HD], a["cache_v"][0, 0, HD:P]).then_inc(vk.cst, 16)
            pool.wait_ge(ffn[0].w_lo, 6 * PAIRS - 2)
            nc.gpsimd.memset(RAW4[:, 1, :, :], 0.0).then_inc(z.padded, 1)

            for n in range(3):
                norm_pool(pool, norm[1], n)

            for q, c in enumerate(STORED):
                j, n = M1[c]
                t0, w = NTILE[n]
                if q == len(STORED) - 3:
                    pool.wait_ge(g.ws, NB + 1)
                    pool.wait_ge(g.w, NB + 1)
                    for i, r in enumerate((R3, R5, R2)):
                        pool.dma_start(grow[i], r[:, :]).then_inc(g.out, 16)
                    pool.dma_start(o[6].rearrange("o b h -> h (o b)"), R4[:, SEQ - 1:SEQ]).then_inc(g.out, 16)
                    pool.dma_start(o[11].rearrange("o b h -> h (o b)"), R4[:, T - 1:T]).then_inc(g.out, 16)
                pool.wait_ge(z.scaled, NORMED.index(c) + 1)
                pool.dma_start(zqk[j - 3, :, t0:t0 + w], ZST[:, q % 4, 0:w]).then_inc(zst[q % 4], 16)
                if q == 2:
                    pool.dma_start(zqk[0, :, :], KTT[:, :]).then_inc(vk.kout, 16)
            flat = lambda ap: ap.rearrange("p h d -> p (h d)")

            def att_load(par, q_col, k_col, v_block):
                s = at_in[par]
                pool.dma_start(QB[:, par], zqk[1:5, :, bass.ds(q_col, P)].rearrange("t p c -> p t c")).then_inc(s, 16)
                pool.dma_start(KW[:, par, 0], zqk[0, :, bass.ds(k_col, 2 * P)]).then_inc(s, 16)
                for g_ in range(2):
                    pool.dma_start(KW[g_ * HD:(g_ + 1) * HD, par, 1], zqk[0, (1 - g_) * HD:(2 - g_) * HD, bass.ds(k_col, 2 * P)]).then_inc(s, 16)
                pool.dma_start(VW[:, par], vtok[bass.ds(v_block, 2)].rearrange("b p f -> p b f")).then_inc(s, 16)

            for q in range(4):
                pool.wait_ge(zst[q], 16 * 3)
            pool.wait_ge(vk.kout, 16)
            pool.wait_ge(vk.tr, 3)
            pool.dma_start(QB[:, 0], zqk[1:5, :, 0:P].rearrange("t p c -> p t c")).then_inc(at_in[0], 16)
            pool.wait_ge(vk.ev, 3)
            pool.dma_start(vtok[0:NB].rearrange("b p f -> p b f"), VTOK[:, 0:NB, :]).then_inc(vk.out, 16)
            pool.dma_start(vtok[NB, 0:DEC], VTOK[0:DEC, NB, :]).then_inc(vk.out, 16)
            for w in range(2):
                wc = slice(w * P, (w + 1) * P)
                pool.dma_start(KW[:, 0, 0, wc], zqk[0, :, 0:P]).then_inc(at_in[0], 16)
                for g_ in range(2):
                    pool.dma_start(KW[g_ * HD:(g_ + 1) * HD, 0, 1, wc], zqk[0, (1 - g_) * HD:(2 - g_) * HD, 0:P]).then_inc(at_in[0], 16)
            pool.wait_ge(vk.out, 32)
            for w in range(2):
                pool.dma_start(VW[:, 0, w], vtok[0]).then_inc(at_in[0], 16)
            att_load(1, P, 0, 0)
            pool.dma_start(flat(o[3][0, 0]), VTOK[:, NB - 1, :]).then_inc(vk.out, 16)
            pool.dma_start(flat(o[8][0, 0, HD:P]), VTOK[0:DEC, NB, :]).then_inc(vk.out, 16)
            pool.dma_start(flat(o[2][0, 0]), KTOK[:, 0, :]).then_inc(vk.out, 16)
            pool.dma_start(flat(o[7][0, 0, HD:P]), KTOK[0:DEC, 1, :]).then_inc(vk.out, 16)

            def stores(h, t):
                for n in range(3):
                    t0, w = NTILE[n]
                    pool.wait_ge(z.ev, h * 12 + (E1 + 3 * t + n + 1))
                    pool.dma_start(zm[bass.ds(h + t * LH, 1), :, t0:t0 + w].rearrange("o p c -> (o p) c"),
                                   ZST[:, (3 * t + n) % 4, 0:w]).then_inc(zst[(3 * t + n) % 4], 16)

            with pool.Fori(0, LH - 1) as h:
                for t in range(4):
                    stores(h, t)
                    if t % 2:
                        pool.wait_ge(t_.ev, h * 4 + (t + 1))
                        i = t // 2
                        att_load(i, h * (2 * P) + (2 + i) * P, h * (2 * P) + (1 + i) * P, h * 2 + (1 + i))
            for t in range(2):
                stores(LH - 1, t)
            pool.wait_ge(t_.ev, 4 * (LH - 1) + 2)
            nc.gpsimd.memset(QB[:, 0, :, DEC:P], 0.0).then_inc(vk.pad, 1)
            nc.gpsimd.memset(KW[:, 0, :, P + DEC:2 * P], 0.0).then_inc(vk.pad, 1)
            pool.wait_ge(vk.pad, 2)
            nc.gpsimd.memset(VW[DEC:P, 0, 1, :], 0.0).then_inc(vk.pad, 1)
            pool.wait_ge(vk.pad, 3)
            pool.dma_start(QB[:, 0, :, 0:DEC], zqk[1:5, :, SEQ:T].rearrange("t p c -> p t c")).then_inc(at_in[0], 16)
            pool.dma_start(KW[:, 0, 0, P:P + DEC], zqk[0, :, SEQ:T]).then_inc(at_in[0], 16)
            for g_ in range(2):
                pool.dma_start(KW[g_ * HD:(g_ + 1) * HD, 0, 1, P:P + DEC], zqk[0, (1 - g_) * HD:(2 - g_) * HD, SEQ:T]).then_inc(at_in[0], 16)
            pool.dma_start(VW[0:DEC, 0, 1, :], vtok[NB, 0:DEC]).then_inc(at_in[0], 16)
            pool.dma_start(VW[:, 0, 0, :], flat(a["cache_v"][0, 0])).then_inc(at_in[0], 16)
            pool.dma_start(CKV[:, :], flat(a["cache_k"][0, 0])).then_inc(vk.cin, 16)
            for t in range(2, 4):
                stores(LH - 1, t)
            pool.wait_ge(vk.cev, 1)
            pool.dma_start(KW[:, 0, 0, 0:P], CKT[:, :]).then_inc(at_in[0], 16)
            for g_ in range(2):
                pool.dma_start(KW[g_ * HD:(g_ + 1) * HD, 0, 1, 0:P], CKT[(1 - g_) * HD:(2 - g_) * HD, :]).then_inc(at_in[0], 16)

            pool.wait_ge(att_lo, 1)

            def m_exponents(b, par, L, loads):
                pool.wait_ge(ma_in[par], loads)
                wait_done(pool, m_.asm, b - 1)
                nc.gpsimd.tensor_tensor(EX[0:L, par, :, 0:L], GU[0:L, par, 0:4, 0:L], MC[0:L, None, 0:L].broadcast_to([L, LH, L]), ALU.add).then_inc(m_.d, 1)
                wait_done(pool, m_.cn, b - 1)
                pool.wait_ge(m_.d, b + 1)
                nc.gpsimd.tensor_tensor(DECAY[:, par, :], GU[:, par, 4:8, L - 1], ONES[:, 0:LH].bitcast(F32), ALU.mult)
                wait_done(pool, m_.den, b - 1)
                nc.gpsimd.tensor_tensor(QWI[:, par, :, 0:L], ZQ[:, par, 0:4, 0:L], GU[:, par, 4:8, 0:L], ALU.mult).then_inc(m_.qw, 1)

            def m_low(b, L, col):
                pool.wait_ge(m_.hi, b + 1)
                nc.gpsimd.tensor_tensor(HL[:, 4:8, bass.ds(col, L)], WN[:, :, 0:L], HH[:, 4:8, bass.ds(col, L)].bitcast(F32), ALU.subtract).then_inc(m_.lo, 1)

            nc.gpsimd.memset(CN[:, :, :], 0.0).then_inc(m_.cz, 1)
            m_exponents(0, 0, P, 32)
            m_exponents(1, 1, P, 32)
            with pool.Fori(0, NB // 2 - 1) as i:
                for par in range(2):
                    m_exponents(i * 2 + 2 + par, par, P, i * 32 + 64)
                    m_low(i * 2 + par, P, i * (2 * P) + par * P)
            m_exponents(NB, 0, DEC, 32 * (NB // 2 + 1))
            m_low(NB - 2, P, (NB - 2) * P)
            pool.wait_ge(m_.cn, NB)
            pool.dma_start(o[4][0, 0].rearrange("h d e -> d h e"), CN[:, :, 0:P]).then_inc(m_.cout, 16)
            pool.dma_start(o[5][0, 0].rearrange("h d -> d h"), CN[:, :, P]).then_inc(m_.cout, 16)
            pool.dma_start(N0C[:, :], a["state_n"][0, 0].rearrange("h d -> d h")).then_inc(m_.c0, 16)
            pool.wait_ge(m_.cout, 32)
            pool.dma_start(CN[:, :, 0:P], a["state_C"][0, 0].rearrange("h d e -> d h e")).then_inc(m_.c0, 16)
            m_low(NB - 1, P, (NB - 1) * P)
            pool.wait_ge(m_.cn, NB + 1)
            m_low(NB, DEC, SEQ)
            pool.dma_start(o[9][0, 0].rearrange("h d e -> d h e"), CN[:, :, 0:P]).then_inc(m_.cout, 16)
            pool.dma_start(o[10][0, 0].rearrange("h d -> d h"), CN[:, :, P]).then_inc(m_.cout, 16)
            pool.wait_ge(m_.cout, 64)
            pool.wait_ge(vk.cst, 32)

            for n in range(3):
                norm_pool(pool, norm[2], n)
            pool.wait_ge(ffn[1].d_mm, 24 * PAIRS)
            pool.dma_start(GF[:, :], a["g_final"][0].partition_broadcast(P)).then_inc(const_in, 16)

        @block.scalar
        def _(act):
            act.wait_ge(const_ops, 6)
            nc.scalar.activation(DT[:, :], DTI[:, :], ACT.Abs).then_inc(dist_abs, 1)
            for b in range(NB + 1):
                L = P if b < NB else DEC
                act.wait_ge(x_tr, 2 * b + 1)
                nc.scalar.activation(X[:, 0:4, b * P:b * P + L], BANK[(2 * b) % 8][:, :].rearrange("p (k c) -> p k c", k=4)[:, :, 0:L], ACT.Copy).then_inc(x_evA, 1)
            act.wait_ge(x_evV, NB + 1)
            act.wait_ge(x_evA, NB + 1)
            act.wait_ge(const_ops, 15)
            norm_act_root(act, norm[0], 0, BANK[4])
            for c in range(4):
                ffn_act_gu_high(act, ffn[0], 0, c, first=True)
            norm_act_high(act, norm[0], 0)
            ffn_act(act, ffn[0], norm[0])

            act.wait_ge(ffn[0].x_add, 24 * LAST + 8)
            norm_act_root(act, norm[1], 0, BANK[4])
            norm_act_high(act, norm[1], 0)
            for j in (1, 2, 3, 4):
                unit_high(act, j % 4, loads_until(j))
            act.wait_ge(const_in, 16 * 12)
            act.wait_ge(ffn[0].x_add, 24 * PAIRS)

            plain = normed = 0
            for c, (j, n) in enumerate(M1):
                t0, w = NTILE[n]
                bank = BANK[c % 4]
                if c in (0, 4):
                    norm_act_root(act, norm[1], 1 + c // 4, BANK[4])
                act.wait_ge(z.mm, c + 1)
                if j == 1:
                    nc.scalar.activation(R1[:, t0:t0 + w], bank[0:LH, 0:w], ACT.Identity, bias=GATE[:, 0:1])
                    nc.scalar.activation(R2[:, t0:t0 + w], bank[32:32 + LH, 0:w], ACT.Identity, bias=GBF[32:32 + LH, 0:1]).then_inc(z.ev, 1)
                    plain += 1
                elif j == 2:
                    nc.scalar.activation(VT[:, t0:t0 + w], bank[:, 0:w], ACT.Copy).then_inc(z.ev, 1)
                    plain += 1
                else:
                    nc.scalar.activation(SQC[:, 0:w], bank[:, 0:w], ACT.Square).then_inc(z.sqc, 1)
                    normed += 1
                    act.wait_ge(z.bd, normed)
                    if normed > 1:
                        act.wait_ge(z.scaled, normed - 1)
                    nc.scalar.activation(RSC[:, 0:w], BANK[5][:, 0:w], ACT.Sqrt, bias=EPSC[:, 0:1], scale=1.0 / HD).then_inc(z.rsc, 1)
                if n == 2:
                    unit_high(act, j % 4, loads_until(j + 4), freed=c + 1)
                if c in (2, 6):
                    norm_act_high(act, norm[1], 1 + c // 4)
                if c == 12:
                    act.wait_ge(z.ev, E1)
                    nc.scalar.activation(R3[:, :], R2[:, :], ACT.Abs).then_inc(g.ab, 1)
                    act.wait_ge(g.ab, 1)
                    nc.scalar.activation(R3[:, :], R3[:, :], ACT.Exp, scale=-1.0).then_inc(g.e, 1)
                    act.wait_ge(g.e, 1)
                    nc.scalar.activation(R3[:, :], R3[:, :], ACT.Ln, bias=1.0).then_inc(g.ln, 1)
                if c == 16:
                    act.wait_ge(g.u, 1)
                    nc.scalar.activation(R2[:, :], R4[:, :], ACT.Exp, scale=-1.0)
                    for b in range(NB + 1):
                        s0, s1 = b * P, min(b * P + P, T)
                        before = GATE[:, 1:2] if b == 0 else GATE[:, 2:3] if b == NB else R4[:, s0 - 1:s0]
                        nc.scalar.activation(R5[:, s0:s1], R3[:, s0:s1], ACT.Exp, bias=before).then_inc(g.w, 1)
                        nc.scalar.activation(R6[:, s0:s1], R1[:, s0:s1], ACT.Exp, bias=R3[:, s1 - 1:s1]).then_inc(g.ws, 1)
            act.wait_ge(g.col, 1)
            nc.scalar.activation(COLS[:, 0:8 * NB], BANK[6][:, 0:8 * NB], ACT.Copy).then_inc(g.colev, 1)
            nc.scalar.activation(COLS[0:DEC, 8 * NB:8 * NB + 8], BANK[6][0:DEC, 8 * NB:8 * NB + 8], ACT.Copy).then_inc(g.colev, 1)
            act.wait_ge(g.out, 16 * 5)
            act.wait_ge(vk.tr, 3)
            nc.scalar.activation(VTOK[:, 0:4, :], BANK[7][:, :].rearrange("p (b c) -> p b c", b=4), ACT.Copy).then_inc(vk.ev, 1)
            nc.scalar.activation(VTOK[:, 4:8, :], BANK[4][:, :].rearrange("p (b c) -> p b c", b=4), ACT.Copy).then_inc(vk.ev, 1)
            nc.scalar.activation(VTOK[0:DEC, NB, :], BANK[5][0:DEC, 0:P], ACT.Copy)
            nc.scalar.activation(KTOK[:, 0, :], BANK[5][:, P:2 * P], ACT.Copy)
            nc.scalar.activation(KTOK[0:DEC, 1, :], BANK[5][0:DEC, 2 * P:3 * P], ACT.Copy).then_inc(vk.ev, 1)

            def att_exps(u):
                act.wait_ge(t_.nmx, u + 1)
                for i in range(4):
                    nc.scalar.activation(SP[:, i, :], SP[:, i, :], ACT.Exp, bias=NMX[:, i:i + 1], accum_out=SUM[:, i:i + 1])
                nc.scalar.activation(ESK[:, :], ESK[:, :], ACT.Exp).then_inc(t_.ex, 1)

            def att_pt(u):
                act.wait_ge(t_.tr, u + 1)
                wait_done(act, t_.o, u)
                nc.scalar.activation(PT[:, 0], BANK[4][:, :].rearrange("p (i q) -> p i q", i=4), ACT.Copy).then_inc(t_.ptA, 1)

            def one_head(h, last=False):
                for t in range(4):
                    for n in range(3):
                        w = NTILE[n][1]
                        i = 3 * t + n
                        act.wait_ge(z.mm, h * 12 + (C1 + i + 1))
                        act.wait_ge(zst[i % 4], h * 48 + 16 * (3 + i // 4))
                        nc.scalar.activation(ZST[:, i % 4, 0:w], BANK[i % 2][:, 0:w], ACT.Sigmoid if t == 3 else ACT.Copy,
                                             scale=float(LD) ** -0.5 if t == 1 else 1.0).then_inc(z.ev, 1)
                        if n == 0:
                            att_exps(h * 4 + t)
                        if n == 1:
                            att_pt(h * 4 + t)
                    if last:
                        continue
                    act.wait_ge(z.mm, h * 12 + (C1 + 3 * t + 3))
                    act.wait_ge(zin[t], h * 16 + 16 * loads_until(12 + t))
                    nc.scalar.activation(WGH[:, t], RAW4[:, t], ACT.Copy).then_inc(z.hi, 1)

            one_head(0)
            with act.Fori(1, LH - 1) as h:
                one_head(h)
            one_head(LH - 1, last=True)
            act.wait_ge(vk.ctr, 1)
            nc.scalar.activation(CKT[:, :], BANK[7][:, 0:P], ACT.Copy).then_inc(vk.cev, 1)
            for u in (2 * NB, 2 * NB + 1):
                att_exps(u)
                att_pt(u)
            act.wait_ge(t_.ev, 2 * NB + 2)
            act.wait_ge(z.mm, C1 + 48)
            nc.scalar.activation(HH[:, 0:4, :], ATT[:, :, :], ACT.Copy).then_inc(att_hi, 1)

            def m_first(b, par, L):
                act.wait_ge(m_.d, b + 1)
                for hh in range(LH):
                    last = nc.scalar.activation(EX[0:L, par, hh, 0:L], EX[0:L, par, hh, 0:L], ACT.Exp, bias=COLS[0:L, bass.ds(b * 8 + hh, 1)])
                last.then_inc(m_.ex, 1)
                act.wait_ge(m_.kvt, b + 1)
                wait_done(act, m_.den, b - 1)
                for hh in range(LH):
                    last = nc.scalar.activation(KWS[0:L, par, hh, :], BANK[3][0:L, hh * P:(hh + 1) * P], ACT.Copy,
                                                scale=COLS[0:L, bass.ds(b * 8 + (4 + hh), 1)])
                last.then_inc(m_.kw, 1)

            def view(bank, L):
                return bank[:, 0:LH * L].rearrange("p (h c) -> p h c", h=LH)

            def m_second(b, L):
                act.wait_ge(m_.den, b + 1)
                wait_done(act, m_.v2, b)
                nc.scalar.activation(DM[:, :, 0:L], view(BANK[6], L), ACT.Abs).then_inc(m_.ad, 1)
                act.wait_ge(m_.w, b + 1)
                nc.scalar.activation(SQM[:, :, 0:L], WN[:, :, 0:L], ACT.Square).then_inc(m_.sq, 1)
                act.wait_ge(m_.dm, b + 1)
                nc.scalar.activation(DM[:, :, 0:L], DM[:, :, 0:L], ACT.Square, scale=EPS ** 0.5).then_inc(m_.d2, 1)

            def m_third(b, L, col):
                act.wait_ge(m_.v2, b + 1)
                nc.scalar.activation(RM[:, :, 0:L], RM[:, :, 0:L], ACT.Sqrt).then_inc(m_.rs, 1)
                act.wait_ge(m_.y, b + 1)
                nc.scalar.activation(HH[:, 4:8, bass.ds(col, L)], WN[:, :, 0:L], ACT.Copy).then_inc(m_.hi, 1)

            m_first(0, 0, P)

            def m_block(b, par, col):
                m_first(b + 1, 1 - par, P)
                m_second(b, P)
                m_third(b, P, col)

            m_block(0, 0, 0)
            with act.Fori(0, NB // 2 - 1) as i:
                m_block(i * 2 + 1, 1, i * (2 * P) + P)
                m_block(i * 2 + 2, 0, i * (2 * P) + 2 * P)
            for b in (NB - 1, NB):
                L = P if b < NB else DEC
                if b < NB:
                    m_first(b + 1, (b + 1) % 2, DEC)
                m_second(b, L)
                m_third(b, L, b * P)

            for t in range(4):
                unit_high(act, t, loads_until(UNITS + 1 + t))
            for t in range(4):
                j = UNITS + 5 + t
                unit_high(act, t, loads_until(j), freed=C1 + 48 + 8 + t + 1)
            act.wait_ge(o_add, 16)
            norm_act_root(act, norm[2], 0, BANK[4])
            norm_act_high(act, norm[2], 0)
            for c in range(4):
                act.wait_ge(z.mm, C1 + 48 + 20 + c + 1)
                ffn_act_gu_high(act, ffn[1], 0, c, first=True)
            act.wait_ge(o_add, 3 * OUT_UNITS)
            ffn_act(act, ffn[1], norm[2])

            for b in range(NB + 1):
                L = P if b < NB else DEC
                for half in range(2):
                    act.wait_ge(fin.tr, 2 * b + half + 1)
                    nc.scalar.activation(JUNK[0:L, (2 * b + half) % 4, :], BANK[(2 * b + half) % 8][0:L, :], ACT.Square, accum_out=FS[0:L, b % 4, half:half + 1]).then_inc(fin.sq, 1)
                act.wait_ge(fin.sum, b + 1)
                nc.scalar.activation(FS[0:L, b % 4, 2:3], FS[0:L, b % 4, 2:3], ACT.Sqrt, bias=EPSC[0:L, 0:1], scale=1.0 / D).then_inc(fin.rs, 1)

        @block.vector
        def _(dve):
            for b in range(NB + 1):
                L = P if b < NB else DEC
                dve.wait_ge(x_tr, 2 * b + 2)
                nc.vector.tensor_copy(X[:, 4:8, b * P:b * P + L], BANK[(2 * b + 1) % 8][:, :].rearrange("p (k c) -> p k c", k=4)[:, :, 0:L]).then_inc(x_evV, 1)
            dve.wait_ge(const_in, 16 * 12)
            nc.vector.tensor_scalar(GQ[:, 0:1], GQ[:, 0:1], float(HD) ** -0.5, None, ALU.mult)
            nc.vector.tensor_scalar(NSINK[:, :], SINK[:, :], -1.0, None, ALU.mult)
            norm_dve(dve, norm[0], 0, 0)
            norm_dve_low(dve, norm[0], 0)
            for c in range(4):
                ffn_dve_gu_low(dve, ffn[0], 0, c)
            ffn_dve(dve, ffn[0], norm[0], 0)

            ffn_dve_x(dve, ffn[0], LAST, 0)
            ffn_dve_x(dve, ffn[0], LAST, 1)
            norm_dve(dve, norm[1], 0, 1)
            ffn_dve_x(dve, ffn[0], LAST, 2, range(4))
            norm_dve_low(dve, norm[1], 0)
            ffn_dve_x(dve, ffn[0], LAST, 2, range(4, KT))
            for j in (1, 2, 3, 4):
                unit_low(dve, j, j % 4)

            normed = stored = 0
            for c, (j, n) in enumerate(M1):
                t0, w = NTILE[n]
                if c in (0, 4):
                    norm_dve(dve, norm[1], 1 + c // 4, 1)
                if j >= 3:
                    if j == 3:
                        dst, gain = KTT[:, t0:t0 + w], GQ[:, 1:2]
                    else:
                        dst, gain = ZST[:, stored % 4, 0:w], GQ[:, 0:1]
                        if stored >= 4:
                            dve.wait_ge(zst[stored % 4], 16 * (stored // 4))
                        stored += 1
                    dve.wait_ge(z.sqc, normed + 1)
                    nc.vector.tensor_scalar(dst, BANK[c % 4][:, 0:w], gain, None, ALU.mult).then_inc(z.zg, 1)
                    normed += 1
                    dve.wait_ge(z.rsc, normed)
                    nc.vector.reciprocal(RSC[:, 0:w], RSC[:, 0:w]).then_inc(z.rc, 1)
                    dve.wait_ge(z.rc, normed)
                    nc.vector.tensor_tensor(dst, dst, RSC[:, 0:w], ALU.mult).then_inc(z.scaled, 1)
                if n == 2:
                    unit_low(dve, j + 4, j % 4)
                if c in (2, 6):
                    norm_dve_low(dve, norm[1], 1 + c // 4)
                if c == 12:
                    nc.vector.memset(R4[:, :], 1.0).then_inc(g.f, 1)
                    dve.wait_ge(g.f, 1)
                    nc.vector.memset(R4[:, 0:T:P], 0.0).then_inc(g.f, 1)
                if c == 14:
                    dve.wait_ge(g.ln, 1)
                    nc.vector.scalar_tensor_tensor(out=R2[:, :], in0=R2[:, :], scalar=0.0, in1=R3[:, :], op0=ALU.min, op1=ALU.subtract).then_inc(g.lf, 1)
                    dve.wait_ge(g.lf, 1)
                    dve.wait_ge(g.f, 2)
                    nc.vector.tensor_tensor_scan(R3[:, :], R4[:, :], R2[:, :], 0.0, ALU.mult, ALU.add).then_inc(g.b, 1)
                    dve.wait_ge(g.b, 1)
                    nc.vector.tensor_tensor_scan(R4[:, 0:SEQ], R2[:, 0:SEQ], R1[:, 0:SEQ], 0.0, ALU.add, ALU.max).then_inc(g.m, 1)
                    nc.vector.tensor_tensor_scan(R4[:, SEQ:T], R2[:, SEQ:T], R1[:, SEQ:T], GATE[:, 2:3], ALU.add, ALU.max).then_inc(g.m, 1)
                    dve.wait_ge(g.m, 2)
                    nc.vector.tensor_tensor(R1[:, :], R1[:, :], R3[:, :], ALU.subtract).then_inc(g.r, 1)
                    dve.wait_ge(g.r, 1)
                    nc.vector.tensor_tensor(R3[:, :], R3[:, :], R4[:, :], ALU.subtract).then_inc(g.u, 1)

            def att_softmax(u, g_, table):
                dve.wait_ge(t_.s, u + 1)
                wait_done(dve, t_.tr, u)
                for i, hl in enumerate(HEAD_ORDER):
                    slope = 2.0 ** -(4 * g_ + hl + 1)
                    last = nc.vector.scalar_tensor_tensor(out=SP[:, i, :], in0=table[:, :], scalar=-slope, in1=BANK[2 + i // 2][:, (i % 2) * 256:(i % 2) * 256 + 256],
                                                          op0=ALU.mult, op1=ALU.add)
                last.then_inc(t_.bias, 1)
                dve.wait_ge(t_.bias, u + 1)
                nc.vector.tensor_reduce(NMX[:, :], SP[:, :, :], AX.X, ALU.max, negate=True).then_inc(t_.nmax, 1)
                dve.wait_ge(t_.nmax, u + 1)
                order = lambda ap: ap[:, 4 * g_:4 * g_ + 4].rearrange("p (a b) -> p b a", b=2)
                nm = NMX[:, :].rearrange("p (b a) -> p b a", b=2)
                nc.vector.tensor_tensor(nm, nm, order(NSINK), ALU.min).then_inc(t_.nmin, 1)
                dve.wait_ge(t_.nmin, u + 1)
                nc.vector.tensor_tensor(ESK[:, :].rearrange("p (b a) -> p b a", b=2), nm, order(SINK), ALU.add).then_inc(t_.nmx, 1)

            def att_normalise(u):
                dve.wait_ge(t_.ex, u + 1)
                nc.vector.tensor_tensor(DEN[:, :], SUM[:, :], ESK[:, :], ALU.add).then_inc(t_.den, 1)
                dve.wait_ge(t_.den, u + 1)
                nc.vector.reciprocal(DEN[:, :], DEN[:, :]).then_inc(t_.rden, 1)
                dve.wait_ge(t_.rden, u + 1)
                for i in range(4):
                    last = nc.vector.tensor_scalar(SP[:, i, :], SP[:, i, :], DEN[:, i:i + 1], None, ALU.mult)
                last.then_inc(t_.p, 1)

            def att_out(u, g_, col, L=P):
                dve.wait_ge(t_.tr, u + 1)
                wait_done(dve, t_.o, u)
                nc.vector.tensor_copy(PT[:, 1], BANK[5][:, :].rearrange("p (i q) -> p i q", i=4)).then_inc(t_.ptV, 1)
                dve.wait_ge(t_.o, u + 1)
                nc.vector.tensor_copy(ATT[:, 2 * g_:2 * g_ + 2, bass.ds(col, L)], BANK[6][:, 0:256].rearrange("p (a q) -> p a q", a=2)[:, :, 0:L]).then_inc(t_.ev, 1)

            def one_head(h, first=False, last=False):
                for t in range(4):
                    u = h * 4 + t
                    att_softmax(u, t % 2, DT0 if first and t < 2 else DT)
                    att_normalise(u)
                    if first and t == 0:
                        dve.wait_ge(vk.out, 16 * 6)
                    att_out(u, t % 2, h * (2 * P) + (t // 2) * P)
                    if not last:
                        unit_low(dve, h * 4 + (12 + t), t)
            dve.wait_ge(const_ops, 15)
            one_head(0, first=True)
            with dve.Fori(1, LH - 1) as h:
                one_head(h)
            one_head(LH - 1, last=True)
            for g_ in range(2):
                att_softmax(2 * NB + g_, g_, DT)
                att_normalise(2 * NB + g_)
                att_out(2 * NB + g_, g_, SEQ, DEC)
            dve.wait_ge(att_hi, 1)
            dve.wait_ge(t_.ev, 2 * NB + 2)
            nc.vector.tensor_tensor(HL[:, 0:4, :], ATT[:, :, :], HH[:, 0:4, :].bitcast(F32), ALU.subtract).then_inc(att_lo, 1)

            def view(bank, L, p=P):
                return bank[0:p, 0:LH * L].rearrange("p (h c) -> p h c", h=LH)

            def m_first(b, par, L):
                dve.wait_ge(m_.kvt, b + 1)
                wait_done(dve, m_.den, b - 1)
                nc.vector.tensor_copy(VM[0:L, par], view(BANK[4], P, L)).then_inc(m_.v, 1)
                dve.wait_ge(m_.ex, b + 1)
                dve.wait_ge(m_.s, b + 1)
                nc.vector.tensor_tensor(ASM[0:L, par, :, 0:L], EX[0:L, par, :, 0:L], view(BANK[2], L, L), ALU.mult).then_inc(m_.asm, 1)

            def m_second(b, par, L, loads):
                dve.wait_ge(m_.num, b + 1)
                dve.wait_ge(mb_in[par], loads)
                wait_done(dve, m_.lo, b)
                nc.vector.tensor_tensor(WN[:, :, 0:L], ZO[:, par, :, 0:L], view(BANK[5], L), ALU.mult).then_inc(m_.w, 1)
                dve.wait_ge(m_.ad, b + 1)
                nc.vector.scalar_tensor_tensor(out=DM[:, :, 0:L], in0=DM[:, :, 0:L], scalar=BOUND, in1=GM[:, par, :, 0:L], op0=ALU.min, op1=ALU.max).then_inc(m_.dm, 1)
                dve.wait_ge(m_.den, b + 1)
                dve.wait_ge(m_.qw, b + 1)
                for hh in range(LH):
                    bank = BANK[7 if hh < 2 else 0]
                    last = nc.vector.scalar_tensor_tensor(out=CN[:, hh, :], in0=CN[:, hh, :], scalar=DECAY[:, par, hh:hh + 1],
                                                          in1=bank[:, (hh % 2) * 256:(hh % 2) * 256 + 256], op0=ALU.mult, op1=ALU.add)
                last.then_inc(m_.cn, 1)

            def m_third(b, L):
                dve.wait_ge(m_.ss, b + 1)
                dve.wait_ge(m_.d2, b + 1)
                nc.vector.scalar_tensor_tensor(out=RM[:, :, 0:L], in0=view(BANK[1], L), scalar=1.0 / LD, in1=DM[:, :, 0:L], op0=ALU.mult, op1=ALU.add).then_inc(m_.v2, 1)
                dve.wait_ge(m_.rs, b + 1)
                nc.vector.reciprocal(RM[:, :, 0:L], RM[:, :, 0:L]).then_inc(m_.rc, 1)
                dve.wait_ge(m_.rc, b + 1)
                for hh in range(LH):
                    last = nc.vector.scalar_tensor_tensor(out=WN[:, hh, 0:L], in0=WN[:, hh, 0:L], scalar=GO[:, hh:hh + 1], in1=RM[:, hh, 0:L], op0=ALU.mult, op1=ALU.mult)
                last.then_inc(m_.y, 1)

            m_first(0, 0, P)
            dve.wait_ge(m_.cz, 1)

            def m_block(b, par, loads):
                m_first(b + 1, 1 - par, P)
                m_second(b, par, P, loads)
                m_third(b, P)

            m_block(0, 0, 32)
            with dve.Fori(0, NB // 2 - 1) as i:
                m_block(i * 2 + 1, 1, i * 32 + 32)
                m_block(i * 2 + 2, 0, i * 32 + 64)
            m_first(NB, 0, DEC)
            m_second(NB - 1, 1, P, 32 * (NB // 2))
            m_third(NB - 1, P)
            dve.wait_ge(m_.c0, 32)
            nc.vector.tensor_copy(CN[:, :, P:2 * P], N0C[:, :, None].broadcast_to([P, LH, P])).then_inc(m_.n0, 1)
            dve.wait_ge(m_.n0, 1)
            m_second(NB, 0, DEC, 32 * (NB // 2 + 1))
            m_third(NB, DEC)

            for t in range(4):
                unit_low(dve, UNITS + 1 + t, t)
            for batch in range(2):
                for n in range(3):
                    if batch == 1 and n == 2:
                        norm_dve(dve, norm[2], 0, 2)
                        norm_dve_low(dve, norm[2], 0)
                    for t in range(4):
                        q = 12 * batch + 4 * n + t
                        dve.wait_ge(z.mm, C1 + 48 + q + 1)
                        nc.vector.tensor_tensor(x_view(4 * batch + t, n), x_view(4 * batch + t, n), BANK[q % 4][:, 0:NTILE[n][1]], ALU.add).then_inc(o_add, 1)
                        if n == 2 and batch == 0:
                            unit_low(dve, UNITS + 5 + t, t)
                        if n == 2 and batch == 1:
                            ffn_dve_gu_low(dve, ffn[1], 0, t)
            ffn_dve(dve, ffn[1], norm[2], 2)
            for n in range(3):
                ffn_dve_x(dve, ffn[1], LAST, n)

            dve.wait_ge(const_in, 16 * 13)
            for b in range(NB + 1):
                L = P if b < NB else DEC
                f = FS[0:L, b % 4]
                dve.wait_ge(fin.sq, 2 * b + 2)
                nc.vector.tensor_tensor(f[:, 2:3], f[:, 0:1], f[:, 1:2], ALU.add).then_inc(fin.sum, 1)
                dve.wait_ge(fin.rs, b + 1)
                nc.vector.reciprocal(f[:, 3:4], f[:, 2:3]).then_inc(fin.rc, 1)
                dve.wait_ge(fin.rc, b + 1)
                if b >= 4:
                    dve.wait_ge(fin_out[b % 4], 16 * (b // 4))
                for half in range(2):
                    c = slice(512 * half, 512 * half + 512)
                    nc.vector.scalar_tensor_tensor(out=YO[0:L, b % 4, c], in0=BANK[(2 * b + half) % 8][0:L, :], scalar=f[:, 3:4], in1=GF[0:L, c],
                                                   op0=ALU.mult, op1=ALU.mult).then_inc(fin.y, 1)

        @block.tensor
        def _(pe):
            pe.wait_ge(const_ops, 11)
            for b in range(NB + 1):
                L = P if b < NB else DEC
                if b % 4 == 0:
                    pe.wait_ge(x_in[b // 4], 16)
                for half in range(2):
                    if b >= 4:
                        pe.wait_ge(x_evV if half else x_evA, b - 3)
                    for k in range(4):
                        f0 = (4 * half + k) * P
                        tr = nc.tensor.transpose(BANK[(2 * b + half) % 8][:, k * P:k * P + L], XIN[0:L, b, f0:f0 + P], IDENT[0:L, 0:L])
                    tr.then_inc(x_tr, 1)
            pe.wait_ge(x_evA, NB + 1)
            pe.wait_ge(x_evV, NB + 1)
            norm_pe(pe, norm[0], 0, BANK[4])
            ffn_pe(pe, ffn[0], norm[0])
            ffn_pe_down(pe, ffn[0], LAST, 0)
            ffn_pe_down(pe, ffn[0], LAST, 1)
            pe.wait_ge(ffn[0].silu, 6 * PAIRS)
            norm_pe(pe, norm[1], 0, BANK[4])
            ffn_pe_down(pe, ffn[0], LAST, 2)

            pe.wait_ge(ffn[0].x_add, 24 * PAIRS)
            pe.wait_ge(ffn[0].mul, 6 * PAIRS)
            bd = []

            def head_sums(c):
                i = NORMED.index(c)
                w = NTILE[M1[c][1]][1]
                pe.wait_ge(z.sqc, i + 1)
                if i:
                    pe.wait_ge(z.rsc, i)
                nc.tensor.matmul(BANK[5][:, 0:w], BD[:, :], SQC[:, 0:w], start=True, stop=True).then_inc(z.bd, 1)

            for c, (j, n) in enumerate(M1):
                if c < 12 and c % 4 == 0:
                    norm_wait(pe, norm[1], n)
                pe.wait_ge(z.lo, j)
                if c >= 4:
                    if c - 4 in PLAIN:
                        pe.wait_ge(z.ev, PLAIN.index(c - 4) + 1)
                    else:
                        pe.wait_ge(z.sqc, NORMED.index(c - 4) + 1)
                        pe.wait_ge(z.zg, NORMED.index(c - 4) + 1)
                unit_chain(pe, n, j % 4, BANK[c % 4])
                if c - 1 in NORMED and c - 1 not in bd:
                    head_sums(c - 1)
                    bd.append(c - 1)
                if c in (3, 7, 11, C1 - 1):
                    head_sums(c)
                    bd.append(c)
                if c in (0, 4):
                    norm_pe(pe, norm[1], 1 + c // 4, BANK[4])
            pe.wait_ge(g.ws, NB + 1)
            for b in range(NB + 1):
                s0, s1 = b * P, min(b * P + P, T)
                for i, r in enumerate((R1, R6)):
                    tr = nc.tensor.transpose(BANK[6][0:s1 - s0, 8 * b + 4 * i:8 * b + 4 * i + 4], r[:, s0:s1], IDENT[0:LH, 0:LH])
            tr.then_inc(g.col, 1)
            pe.wait_ge(z.scaled, len(NORMED))
            for b in range(NB + 1):
                s0, s1 = b * P, min(b * P + P, T)
                bank = BANK[(7, 4, 5)[b // 4]]
                tr = nc.tensor.transpose(bank[0:s1 - s0, (b % 4) * P:(b % 4) * P + P], VT[:, s0:s1], IDENT[:, :])
                if b % 4 == 3:
                    tr.then_inc(vk.tr, 1)
            nc.tensor.transpose(BANK[5][:, P:2 * P], KTT[:, SEQ - P:SEQ], IDENT[:, :])
            nc.tensor.transpose(BANK[5][0:DEC, 2 * P:3 * P], KTT[:, SEQ:T], IDENT[:, :]).then_inc(vk.tr, 1)
            pe.wait_ge(z.zg, len(NORMED))
            pe.wait_ge(z.sqc, len(NORMED))
            pe.wait_ge(z.ev, E1)
            pe.wait_ge(vk.ev, 3)
            pe.wait_ge(g.colev, 2)

            def att_scores(u, par, g_, loads):
                pe.wait_ge(at_in[par], loads)
                wait_done(pe, t_.bias, u)
                for i, hl in enumerate(HEAD_ORDER):
                    po = hl % 2
                    rows = slice(po * HD, po * HD + HD)
                    mm = nc.tensor.matmul(BANK[2 + i // 2][:, (i % 2) * 256:(i % 2) * 256 + 256], QB[rows, par, 2 * g_ + hl // 2, :],
                                          KW[rows, par, 0 if g_ == po else 1, :], start=True, stop=True)
                mm.then_inc(t_.s, 1)

            def att_transposes(u):
                pe.wait_ge(t_.p, u + 1)
                wait_done(pe, t_.ptA, u)
                wait_done(pe, t_.ptV, u)
                for w in range(2):
                    for i in range(4):
                        tr = nc.tensor.transpose(BANK[4 + w][:, i * P:(i + 1) * P], SP[:, i, w * P:(w + 1) * P], IDENT[:, :])
                tr.then_inc(t_.tr, 1)

            def att_values(u, par, g_):
                pe.wait_ge(t_.ptA, u + 1)
                pe.wait_ge(t_.ptV, u + 1)
                wait_done(pe, t_.ev, u)
                for po in range(2):
                    for w in range(2):
                        mm = nc.tensor.matmul(BANK[6][po * HD:po * HD + HD, 0:256], VW[:, par, w, g_ * HD:g_ * HD + HD],
                                              PT[:, w, 2 * po:2 * po + 2, :], start=(w == 0), stop=(w == 1))
                mm.then_inc(t_.o, 1)

            def one_head(h):
                for t in range(4):
                    u, par, g_ = h * 4 + t, t // 2, t % 2
                    att_scores(u, par, g_, h * 80 + (80 if par else 144))
                    pe.wait_ge(z.lo, h * 4 + (8 + t))
                    for n in range(3):
                        i = 3 * t + n
                        pe.wait_ge(z.ev, h * 12 + (E1 + i - 1))
                        unit_chain(pe, n, t, BANK[i % 2])
                        if n == 1:
                            att_transposes(u)
                    att_values(u, par, g_)

            one_head(0)
            with pe.Fori(1, LH) as h:
                one_head(h)
            pe.wait_ge(vk.cin, 16)
            nc.tensor.transpose(BANK[7][:, 0:P], CKV[:, :], IDENT[:, :]).then_inc(vk.ctr, 1)
            for g_ in range(2):
                att_scores(2 * NB + g_, 0, g_, 144 + 3 * 80 + 144)
                att_transposes(2 * NB + g_)
                att_values(2 * NB + g_, 0, g_)

            def m_first(b, par, L, loads):
                pe.wait_ge(ma_in[par], loads)
                wait_done(pe, m_.kw, b)
                wait_done(pe, m_.v, b)
                for bank, first in ((3, 4), (4, 8)):
                    for hh in range(LH):
                        tr = nc.tensor.transpose(BANK[bank][0:L, hh * P:(hh + 1) * P], ZQ[:, par, first + hh, 0:L], IDENT[:, :])
                tr.then_inc(m_.kvt, 1)
                wait_done(pe, m_.asm, b)
                for hh in range(LH):
                    mm = nc.tensor.matmul(BANK[2][0:L, hh * L:(hh + 1) * L], ZQ[:, par, 4 + hh, 0:L], ZQ[:, par, hh, 0:L], start=True, stop=True)
                mm.then_inc(m_.s, 1)

            def m_second(b, par, L):
                pe.wait_ge(m_.kw, b + 1)
                pe.wait_ge(m_.v, b + 1)
                wait_done(pe, m_.cn, b)
                for hh in range(LH):
                    bank, c = BANK[7 if hh < 2 else 0], (hh % 2) * 256
                    nc.tensor.matmul(bank[:, c:c + P], KWS[0:L, par, hh, :], VM[0:L, par, hh, :], start=True, stop=True)
                    nc.tensor.matmul(bank[:, c + P:c + 2 * P], KWS[0:L, par, hh, :], ONES[0:L, :], start=True, stop=True)
                pe.wait_ge(m_.asm, b + 1)
                pe.wait_ge(m_.qw, b + 1)
                wait_done(pe, m_.w, b)
                for hh in range(LH):
                    out = BANK[5][:, hh * L:(hh + 1) * L]
                    nc.tensor.matmul(out, VM[0:L, par, hh, :], ASM[0:L, par, hh, 0:L], start=True, stop=False)
                    mm = nc.tensor.matmul(out, CN[:, hh, 0:P], QWI[:, par, hh, 0:L], start=False, stop=True)
                mm.then_inc(m_.num, 1)
                wait_done(pe, m_.ad, b)
                for hh in range(LH):
                    out = BANK[6][:, hh * L:(hh + 1) * L]
                    nc.tensor.matmul(out, ONES[0:L, :], ASM[0:L, par, hh, 0:L], start=True, stop=False)
                    mm = nc.tensor.matmul(out, CN[:, hh, P:2 * P], QWI[:, par, hh, 0:L], start=False, stop=True)
                mm.then_inc(m_.den, 1)

            def m_third(b, L):
                pe.wait_ge(m_.sq, b + 1)
                wait_done(pe, m_.v2, b)
                nc.tensor.matmul(BANK[1][:, 0:LH * L], ONES[:, :], SQM[:, :, 0:L], start=True, stop=True).then_inc(m_.ss, 1)

            pe.wait_ge(z.ev, E1 + 48)
            pe.wait_ge(t_.ev, 2 * NB + 2)
            m_first(0, 0, P, 32)
            pe.wait_ge(m_.cz, 1)

            def m_block(b, par, next_loads):
                m_first(b + 1, 1 - par, P, next_loads)
                m_second(b, par, P)
                m_third(b, P)

            m_block(0, 0, 32)
            with pe.Fori(0, NB // 2 - 1) as i:
                m_block(i * 2 + 1, 1, i * 32 + 64)
                m_block(i * 2 + 2, 0, i * 32 + 64)
            m_first(NB, 0, DEC, 32 * (NB // 2 + 1))
            m_second(NB - 1, 1, P)
            m_third(NB - 1, P)
            pe.wait_ge(m_.n0, 1)
            m_second(NB, 0, DEC)
            m_third(NB, DEC)

            pe.wait_ge(m_.lo, NB + 1)
            pe.wait_ge(m_.v2, NB + 1)
            for q in range(3 * OUT_UNITS):
                batch, n, t = q // 12, q % 12 // 4, q % 4
                if n == 0:
                    pe.wait_ge(z.lo, UNITS + 1 + 4 * batch + t)
                if q >= 4:
                    pe.wait_ge(o_add, q - 3)
                unit_chain(pe, n, t, BANK[q % 4])
                if q == 19:
                    norm_pe(pe, norm[2], 0, BANK[4])
            pe.wait_ge(o_add, 3 * OUT_UNITS)
            ffn_pe(pe, ffn[1], norm[2])
            for n in range(3):
                ffn_pe_down(pe, ffn[1], LAST, n)

            pe.wait_ge(ffn[1].x_add, 24 * PAIRS)
            for b in range(NB + 1):
                L = P if b < NB else DEC
                if b >= 4:
                    pe.wait_ge(fin.y, 2 * (b - 3))
                for half in range(2):
                    for k in range(4):
                        tr = nc.tensor.transpose(BANK[(2 * b + half) % 8][0:L, k * P:(k + 1) * P], X[:, 4 * half + k, b * P:b * P + L], IDENT[:, :])
                    tr.then_inc(fin.tr, 1)


_INS = ["x_prompt", "x_sample", "cache_k", "cache_v", "state_C", "state_n", "state_m", "g_ffn1", "w1_gate", "w1_up", "w1_down",
        "g_mix", "w_in", "b_igate", "b_fgate", "g_q", "g_k", "attn_sinks", "g_lstm_out", "w_out", "g_ffn2", "w2_gate", "w2_up",
        "w2_down", "g_final"]
_ROWS = (1, 1, P, KV, HD)
_OUTS = [(1, SEQ, D), (1, DEC, D),
         _ROWS, _ROWS, (1, 1, LH, LD, LD), (1, 1, LH, LD), (1, 1, LH),
         _ROWS, _ROWS, (1, 1, LH, LD, LD), (1, 1, LH, LD), (1, 1, LH)]


def kernel(**inputs):
    import numpy as _np
    import concourse.bacc as _bacc
    from concourse import mybir as _mybir
    from concourse.bass_utils import run_bass_kernel_spmd as _run

    nc = _bacc.Bacc("TRN2", target_bir_lowering=False, num_devices=1)
    arrays, ins = {}, {}
    for name in _INS:
        x = _np.ascontiguousarray(inputs[name])
        arrays[f"in_{name}"] = x
        ins[name] = nc.dram_tensor(f"in_{name}", x.shape, _mybir.dt.from_np(x.dtype), kind="ExternalInput").ap()
    outs = [nc.dram_tensor(f"out_{i}", shape, _mybir.dt.float32, kind="ExternalOutput").ap() for i, shape in enumerate(_OUTS)]
    build(nc, ins, outs)
    r = _run(nc, [arrays], core_ids=[0])
    return tuple(r.results[0][f"out_{i}"] for i in range(len(_OUTS)))
```
